# Optimizing a Trainium2 kernel written in Bass

```python
import jax
import jax.numpy as jnp
from jax import lax
import numpy as np

D_MODEL = 1024
BATCH = 1
SEQ = 512
DEPTH = 2
DEC_BATCH = 1
DEC_SEQ = 512
PAST_LEN = 128

HEAD_DIM = 64
A_HEADS = 8
A_KV_HEADS = 2
B_HEADS = 4
B_KV_HEADS = 2
C_HEADS = 4
A_WIDTH = A_HEADS * HEAD_DIM
B_WIDTH = B_HEADS * HEAD_DIM
C_WIDTH = C_HEADS * HEAD_DIM
MIX_WIDTH = A_WIDTH + B_WIDTH + C_WIDTH
IN_SPLITS = (A_HEADS * HEAD_DIM, A_KV_HEADS * HEAD_DIM, A_KV_HEADS * HEAD_DIM,
             B_HEADS * HEAD_DIM, B_KV_HEADS * HEAD_DIM, B_KV_HEADS * HEAD_DIM,
             C_HEADS * HEAD_DIM, C_HEADS * HEAD_DIM, C_HEADS * HEAD_DIM)
IN_WIDTH = (A_HEADS + 2 * A_KV_HEADS + B_HEADS + 2 * B_KV_HEADS + 3 * C_HEADS) * HEAD_DIM
WINDOW = 128
BLOCK = 128
GRID_W = 64
NA_ROWS = 8
NA_COLS = 16
N_EXPERTS = 16
CAPACITY_FACTOR = 2
D_FF_EXPERT = 1024
ROPE_THETA = 10000.0
EPS = 1e-6
NEG_INF = -1e30

kernel_name = "hybrid_parallel_heads_ec_encoder"

def rmsnorm(x, g):
    xf = x.astype(jnp.float32)
    y = xf * lax.rsqrt(jnp.mean(xf * xf, axis=-1, keepdims=True) + EPS)
    return (y * g.astype(jnp.float32)).astype(x.dtype)

def rope_cos_sin(pos, dim):
    inv = ROPE_THETA ** (-jnp.arange(0, dim, 2, dtype=jnp.float32) / dim)
    ang = pos.astype(jnp.float32)[:, None] * inv[None, :]
    ang = jnp.concatenate([ang, ang], axis=-1)
    return jnp.cos(ang), jnp.sin(ang)

def apply_rope(x, cos, sin):
    xf = x.astype(jnp.float32)
    x1, x2 = jnp.split(xf, 2, axis=-1)
    rot = jnp.concatenate([-x2, x1], axis=-1)
    return (xf * cos[:, None, :] + rot * sin[:, None, :]).astype(x.dtype)

def apply_axial_rope(x):
    s = x.shape[1]
    t = jnp.arange(s)
    half = x.shape[-1] // 2
    cr, sr = rope_cos_sin(t // GRID_W, half)
    cc, sc = rope_cos_sin(t % GRID_W, half)
    xr, xc = jnp.split(x, 2, axis=-1)
    return jnp.concatenate([apply_rope(xr, cr, sr), apply_rope(xc, cc, sc)], axis=-1)

def window_sink_attention(q, k, v, sink):
    b, s, hq, dh = q.shape
    kvh = k.shape[2]
    g = hq // kvh
    q = q.reshape(b, s, kvh, g, dh)
    pad = ((0, 0), (WINDOW, WINDOW), (0, 0), (0, 0))
    kp = jnp.pad(k, pad)
    vp = jnp.pad(v, pad)
    span = BLOCK + 2 * WINDOW
    scale = dh ** -0.5
    sink_l = sink.astype(jnp.float32).reshape(kvh, g)

    def one_block(i):
        start = i * BLOCK
        qb = lax.dynamic_slice_in_dim(q, start, BLOCK, axis=1)
        kb = lax.dynamic_slice_in_dim(kp, start, span, axis=1)
        vb = lax.dynamic_slice_in_dim(vp, start, span, axis=1)
        qpos = start + jnp.arange(BLOCK)
        kpos = start - WINDOW + jnp.arange(span)
        ok = (jnp.abs(qpos[:, None] - kpos[None, :]) <= WINDOW) & (kpos[None, :] >= 0) & (kpos[None, :] < s)
        sc = jnp.einsum('bqkgd,bnkd->bkgqn', qb, kb).astype(jnp.float32) * scale
        sc = jnp.where(ok, sc, NEG_INF)
        sk = jnp.broadcast_to(sink_l[None, :, :, None, None], sc.shape[:-1] + (1,))
        p = jax.nn.softmax(jnp.concatenate([sc, sk], axis=-1), axis=-1)[..., :span]
        o = jnp.einsum('bkgqn,bnkd->bqkgd', p.astype(v.dtype), vb)
        return o.reshape(b, BLOCK, hq * dh)

    out = lax.map(one_block, jnp.arange(s // BLOCK))
    return jnp.moveaxis(out, 0, 1).reshape(b, s, hq * dh)

def dense_block_attention(q, k, v):
    b, s, hq, dh = q.shape
    kvh = k.shape[2]
    g = hq // kvh
    q = q.reshape(b, s, kvh, g, dh)
    scale = dh ** -0.5

    def one_block(i):
        qb = lax.dynamic_slice_in_dim(q, i * BLOCK, BLOCK, axis=1)
        sc = jnp.einsum('bqkgd,bnkd->bkgqn', qb, k).astype(jnp.float32) * scale
        p = jax.nn.softmax(sc, axis=-1)
        o = jnp.einsum('bkgqn,bnkd->bqkgd', p.astype(v.dtype), v)
        return o.reshape(b, BLOCK, hq * dh)

    out = lax.map(one_block, jnp.arange(s // BLOCK))
    return jnp.moveaxis(out, 0, 1).reshape(b, s, hq * dh)

def neighbourhood_attention(q, k, v, rpb):
    b, s, h, dh = q.shape
    rows = s // GRID_W
    kh = min(NA_ROWS, rows)
    kw = NA_COLS
    n_keys = kh * kw
    r = jnp.arange(rows)
    c = jnp.arange(GRID_W)
    rs = jnp.clip(r - kh // 2, 0, rows - kh)
    cs = jnp.clip(c - kw // 2, 0, GRID_W - kw)
    krow = rs[:, None] + jnp.arange(kh)[None, :]
    kcol = cs[:, None] + jnp.arange(kw)[None, :]
    idx = (krow[:, None, :, None] * GRID_W + kcol[None, :, None, :]).reshape(rows, GRID_W, n_keys)
    dr = krow - r[:, None] + (NA_ROWS - 1)
    dc = kcol - c[:, None] + (NA_COLS - 1)
    bias = rpb[:, dr[:, None, :, None], dc[None, :, None, :]]
    bias = jnp.moveaxis(bias.reshape(h, rows, GRID_W, n_keys), 1, 0)
    scale = dh ** -0.5

    def one_row(args):
        ri, idx_r, bias_r = args
        qr = lax.dynamic_slice_in_dim(q, ri * GRID_W, GRID_W, axis=1)
        flat = idx_r.reshape(-1)
        kg = jnp.take(k, flat, axis=1).reshape(b, GRID_W, n_keys, h, dh)
        vg = jnp.take(v, flat, axis=1).reshape(b, GRID_W, n_keys, h, dh)
        sc = jnp.einsum('bqhd,bqnhd->bhqn', qr, kg).astype(jnp.float32) * scale
        sc = sc + bias_r[None].astype(jnp.float32)
        p = jax.nn.softmax(sc, axis=-1)
        o = jnp.einsum('bhqn,bqnhd->bqhd', p.astype(v.dtype), vg)
        return o.reshape(b, GRID_W, h * dh)

    out = lax.map(one_row, (jnp.arange(rows), idx, bias))
    return jnp.moveaxis(out, 0, 1).reshape(b, s, h * dh)

def token_mixers(hn, w_in, sink, q_gain, k_gain, rpb, g_grp, w_out):
    b, s, _ = hn.shape
    proj = jnp.dot(hn, w_in)
    offsets = np.cumsum(IN_SPLITS)[:-1].tolist()
    qa, ka, va, qb, kb, vb, qc, kc, vc = jnp.split(proj, offsets, axis=-1)
    heads = lambda t: t.reshape(b, s, -1, HEAD_DIM)
    cos, sin = rope_cos_sin(jnp.arange(s), HEAD_DIM)
    oa = window_sink_attention(apply_rope(heads(qa), cos, sin), apply_rope(heads(ka), cos, sin), heads(va), sink)
    qb_ = apply_axial_rope(rmsnorm(heads(qb), q_gain))
    kb_ = apply_axial_rope(rmsnorm(heads(kb), k_gain))
    ob = dense_block_attention(qb_, kb_, heads(vb))
    oc = neighbourhood_attention(heads(qc), heads(kc), heads(vc), rpb)
    merged = jnp.concatenate([
        rmsnorm(oa, g_grp[:A_WIDTH]),
        rmsnorm(ob, g_grp[A_WIDTH:A_WIDTH + B_WIDTH]),
        rmsnorm(oc, g_grp[A_WIDTH + B_WIDTH:]),
    ], axis=-1)
    return jnp.dot(merged, w_out)

def expert_choice_ffn(hn, w_router, w_gate, w_up, w_down):
    b, s, d = hn.shape
    n = b * s
    cap = CAPACITY_FACTOR * n // N_EXPERTS
    hf = hn.reshape(n, d)
    aff = jax.nn.softmax(jnp.dot(hf, w_router).astype(jnp.float32), axis=-1)
    gate, idx = lax.top_k(aff.T, cap)
    xe = jnp.take(hf, idx, axis=0)
    hid = jax.nn.silu(jnp.einsum('ecd,edf->ecf', xe, w_gate)) * jnp.einsum('ecd,edf->ecf', xe, w_up)
    ye = jnp.einsum('ecf,efd->ecd', hid, w_down) * gate[..., None].astype(hn.dtype)
    y = jnp.zeros((n, d), hn.dtype).at[idx.reshape(-1)].add(ye.reshape(-1, d))
    return y.reshape(b, s, d)

def encoder_layer(x, c, w_ada, b_ada, g_mix, w_in, sink, q_gain, k_gain, rpb, g_grp, w_out,
                  g_ffn, w_router, w_gate, w_up, w_down):
    mod = jnp.dot(jax.nn.silu(c), w_ada) + b_ada
    sh1, sc1, gt1, sh2, sc2, gt2 = [m[:, None, :] for m in jnp.split(mod, 6, axis=-1)]
    hn = rmsnorm(x, g_mix) * (1 + sc1) + sh1
    x = x + gt1 * token_mixers(hn, w_in, sink, q_gain, k_gain, rpb, g_grp, w_out)
    hn = rmsnorm(x, g_ffn) * (1 + sc2) + sh2
    x = x + gt2 * expert_choice_ffn(hn, w_router, w_gate, w_up, w_down)
    return x

def setup_inputs(seed: int = 0) -> dict:
    key = jax.random.key(seed)
    ks = jax.random.split(key, 24)
    f32 = jnp.float32
    nrm = lambda k, shape, scale: jax.random.normal(k, shape, f32) * scale
    gain = lambda k, shape: 1.0 + 0.02 * jax.random.normal(k, shape, f32)
    D = D_MODEL
    return {
        "x_prompt": nrm(ks[0], (BATCH, SEQ, D), 1.0),
        "x_sample": nrm(ks[1], (DEC_BATCH, DEC_SEQ, D), 1.0),
        "c_prompt": nrm(ks[2], (BATCH, D), 1.0),
        "c_sample": nrm(ks[3], (DEC_BATCH, D), 1.0),
        "w_ada": nrm(ks[4], (DEPTH, D, 6 * D), D ** -0.5),
        "b_ada": nrm(ks[5], (DEPTH, 6 * D), 0.02),
        "g_mix": gain(ks[6], (DEPTH, D)),
        "w_in": nrm(ks[7], (DEPTH, D, IN_WIDTH), D ** -0.5),
        "sink": nrm(ks[8], (DEPTH, A_HEADS), 1.0),
        "q_gain": gain(ks[9], (DEPTH, HEAD_DIM)),
        "k_gain": gain(ks[10], (DEPTH, HEAD_DIM)),
        "rpb": nrm(ks[11], (DEPTH, C_HEADS, 2 * NA_ROWS - 1, 2 * NA_COLS - 1), 0.5),
        "g_grp": gain(ks[12], (DEPTH, MIX_WIDTH)),
        "w_out": nrm(ks[13], (DEPTH, MIX_WIDTH, D), MIX_WIDTH ** -0.5),
        "g_ffn": gain(ks[14], (DEPTH, D)),
        "w_router": nrm(ks[15], (DEPTH, D, N_EXPERTS), D ** -0.5),
        "w_gate": nrm(ks[16], (DEPTH, N_EXPERTS, D, D_FF_EXPERT), D ** -0.5),
        "w_up": nrm(ks[17], (DEPTH, N_EXPERTS, D, D_FF_EXPERT), D ** -0.5),
        "w_down": nrm(ks[18], (DEPTH, N_EXPERTS, D_FF_EXPERT, D), D_FF_EXPERT ** -0.5),
        "g_final": gain(ks[19], (D,)),
    }

def reference(x_prompt, x_sample, c_prompt, c_sample, w_ada, b_ada, g_mix, w_in, sink, q_gain, k_gain,
              rpb, g_grp, w_out, g_ffn, w_router, w_gate, w_up, w_down, g_final):
    def trunk(x, c):
        for i in range(DEPTH):
            x = encoder_layer(x, c, w_ada[i], b_ada[i], g_mix[i], w_in[i], sink[i], q_gain[i], k_gain[i],
                              rpb[i], g_grp[i], w_out[i], g_ffn[i], w_router[i], w_gate[i], w_up[i], w_down[i])
        return rmsnorm(x, g_final)

    y_prompt = trunk(x_prompt, c_prompt)
    y_sample = trunk(x_sample, c_sample)
    return (y_prompt, y_sample)


_drawn_inputs = setup_inputs


def setup_inputs(seed=0):
    import zlib

    import numpy as np

    out = dict(_drawn_inputs(seed))
    spreads = {}
    factors = {'sink': 8.0, 'q_gain': 4.751, 'k_gain': 7.979, 'g_final': 2.792}
    for name, (base, spread) in spreads.items():
        noise = np.random.default_rng([zlib.crc32(name.encode()), seed]).standard_normal(out[name].shape)
        drawn = base * np.exp(spread * noise) if base else spread * noise
        out[name] = jnp.asarray(drawn.astype(out[name].dtype))
    for name, factor in factors.items():
        out[name] = (out[name] * factor).astype(out[name].dtype)
    return out
```

```python
import concourse.bass as bass
from concourse import mybir
from contextlib import ExitStack

LAYERS, SEQS, SEQ, D = 2, 2, 512, 1024
HD = 64
P = 128
KT = D // P
TILES = SEQ // P
MIX_CHUNKS = 4
ADA = 6 * D
EXPERTS, CAP = 16, 64
GROUP = 4
GROUPS = EXPERTS // GROUP
RING = 6
GRID, NA_ROWS, ROW_OFF, COL_OFF = 64, 8, 15, 31
TURNS = ADA // 512 // RING + 1 + EXPERTS
EPOCHS = 1 + SEQS + 1 + GROUPS
EPS = 1e-6
BIG = 1e30
UNITS = 16 * TILES
T_LAG, V_LAG = 2, 3

C_ID, C_MASKA, C_MASKC, C_ROPE, C_END = 0, 128, 512, 576, 1600
V_SH1, V_SC1, V_SH2, V_SC2, V_GMIX, V_GFFN, V_GGRP, V_END = 0, 8, 16, 24, 32, 40, 48, 56


def unit(u):
    if u < 8:
        j, g = u // 2, u % 2
        h = 4 * g + j
        return "A", j, g, 0, g * HD, h * HD, h
    if u < 12:
        j, g = (u - 8) // 2, u % 2
        h = 2 * g + j
        return "B", 4 + j, g, 1, 128 + g * HD, 512 + h * HD, 8 + h
    j, g = (u - 12) // 2, u % 2
    h = 2 * j + g
    return "C", 6 + j, g, 2 + j, 256 + h * HD, 768 + h * HD, 12 + h


def keys(i, u):
    if u < 8:
        lo, hi = max(i - 1, 0), min(i + 1, TILES - 1)
        return lo, hi - lo + 1
    return 0, TILES


AFTER = [(16 + V_LAG - 1, "finish"), (23, "merged_0"), (24, "merged_1"), (25, "out_0"), (27, "out_1"),
         (28, "norm"), (32, "normed_0"), (33, "normed_1"), (35, "router")]
SLOTS = 16 * (TILES - 1) + AFTER[-1][0] + 1


def schedule():
    out = []
    for k in range(SLOTS):
        out.append(("slot", k // 16, k))
        for i in range(TILES):
            out += [(name, i, k) for at, name in AFTER if 16 * i + at == k]
    return out


def trunk(nc, x, c, w_ada, b_ada, g_mix, w_in, sink, q_gain, k_gain, rpb, g_grp, w_out, g_ffn, w_router,
          w_gate, w_up, w_down, g_final, consts, y):
    f32, u32 = mybir.dt.float32, mybir.dt.uint32
    ALU, ACT, AX = mybir.AluOpType, mybir.ActivationFunctionType, mybir.AxisListType
    ctx = ExitStack()
    with ctx:
        def sb(name, shape, dt=f32):
            return ctx.enter_context(nc.sbuf_tensor(name, shape, dt))

        def sem(name):
            return ctx.enter_context(nc.semaphore(name))

        x_d = nc.dram_tensor("residual", [SEQS * SEQ, D], f32).ap()
        xn_d = nc.dram_tensor("normed", [SEQS * SEQ, D], f32).ap()
        mod_d = nc.dram_tensor("modulation", [SEQS, ADA], f32).ap()
        skew_d = nc.dram_tensor("bias_rows", [4 * ROW_OFF, GRID, 128], f32).ap()

        ring = [sb(f"ring{j}", [P, KT, 512]) for j in range(RING)]
        con = sb("con", [P, C_END])
        ident = con[:, C_ID:C_ID + P]
        mask_a = con[:, C_MASKA:C_MASKA + 3 * P]
        mask_c = con[:, C_MASKC:C_MASKC + GRID]
        silu_c = sb("silu_c", [P, KT, SEQS])
        vec = sb("vec", [P, V_END])
        mod_e = sb("mod_e", [P, 2, KT, SEQS])
        gate1 = sb("gate1", [P, D])
        gate2 = sb("gate2", [P, D])
        bias_c = sb("bias_c", [P, 4, 14, GRID])
        router = sb("router_w", [P, KT, EXPERTS])
        gain_b = sb("gain_b", [P, 6, HD])
        nsink = sb("nsink", [P, 8])
        sinks = sb("sinks", [P, 8])
        neg_half = sb("neg_half", [P, 8])
        aff = sb("aff", [P, TILES, SEQS, 32])
        qT = sb("qT", [P, 8, SEQ])
        kT = sb("kT", [P, 4, SEQ])
        V = sb("V", [P, TILES, 512])
        X = [sb(f"X{i}", [P, D]) for i in range(TILES)]
        xn = sb("xn", [P, D])
        hT = [sb(f"hT{i}", [P, KT, P]) for i in range(2)]
        nat = sb("nat", [P, 1536])
        og = nat[:, 0:D]
        pbuf = sb("pbuf", [P, 5, 512])
        stat = sb("stat", [P, 32])
        smin = sb("smin", [P, 2, 16])
        ssum = sb("ssum", [P, 2, 16])
        rinv = sb("rinv", [P, 16])
        soft = sb("soft", [P, 20])
        hidT = kT[:, 0:2, :].rearrange("p a (b t) -> p (a b) t", t=P)
        idx_t = sb("idx_t", [P, EXPERTS], u32)
        idx_f = sb("idx_f", [P, EXPERTS])
        gate_t = sb("gate_t", [P, EXPERTS])
        idx_now = [sb(f"idx_now{j}", [P, 1], u32) for j in range(GROUP)]
        gate_now = sb("gate_now", [P, GROUP])
        bank = [ctx.enter_context(nc.psum_tensor(f"bank{i}", [P, 512], f32)) for i in range(8)]

        slot_loaded = [sem(f"slot_loaded{j}") for j in range(RING)]
        slot_free = [sem(f"slot_free{j}") for j in range(RING)]
        started = sem("started")
        consts_in, passed = sem("consts_in"), sem("passed")
        arrived, released = sem("arrived"), sem("released")
        layer_in = sem("layer_in")
        skew_in, skew_out, bias_in = sem("skew_in"), sem("skew_out"), sem("bias_in")
        mod_out, vec_in = sem("mod_out"), sem("vec_in")
        x_in = [sem(f"x_in{i}") for i in range(TILES)]
        x_out, xn_out = sem("x_out"), sem("xn_out")
        gathered = [sem(f"gathered{j}") for j in range(GROUP)]
        scattered = sem("scattered")
        gate2_in = sem("gate2_in")
        y_out = sem("y_out")

        cleared = []

        def part(name):
            cleared.append(sem(name))
            return cleared[-1]

        dve_done = part("dve_done")
        act_done = part("act_done")
        var_ready = part("var_ready")
        rstd_ready = part("rstd_ready")
        pad_ready = part("pad_ready")
        ada_mm, ada_added = part("ada_mm"), part("ada_added")
        vec_turned, vec_ready = part("vec_turned"), part("vec_ready")
        xn_ready, h_turned, h_ready = part("xn_ready"), part("h_turned"), part("h_ready")
        proj_done, proj_read_v, proj_read_s = part("proj_done"), part("proj_read_v"), part("proj_read_s")
        nat_ready, qk_turned, qk_copied = part("nat_ready"), part("qk_turned"), part("qk_copied")
        kc_ready = part("kc_ready")
        scored, biased, probs_ready = part("scored"), part("biased"), part("probs_ready")
        p_turned, pt_by_s, pt_by_v, pv_done = part("p_turned"), part("pt_by_s"), part("pt_by_v"), part("pv_done")
        sink_arg, sink_exp, heads_read, merged = part("sink_arg"), part("sink_exp"), part("heads_read"), part("merged")
        side_full, side_free = part("side_full"), part("side_free")
        x_new, xn_new = part("x_new"), part("xn_new")
        logit_max, aff_exp = part("logit_max"), part("aff_exp")
        route_turned, route_ready = part("route_turned"), part("route_ready")
        idx_ready = part("idx_ready")
        xe_turned, xe_ready = part("xe_turned"), part("xe_ready")
        gu_done, silu_done, hid_ready = part("gu_done"), part("silu_done"), part("hid_ready")
        hid_turned, hid_copied = part("hid_turned"), part("hid_copied")
        y_done, y_scaled = part("y_done"), part("y_scaled")
        nums = [s.num for s in cleared]
        assert nums == list(range(nums[0], nums[0] + len(nums)))

        def settle(eng):
            eng.sem_inc(passed, 1)

        def barrier(eng, n):
            eng.drain().then_inc(arrived, 1)
            eng.wait_ge(released, n)
            settle(eng)

        class Chain:
            def __init__(self, eng, done):
                self.eng, self.done, self.n = eng, done, 0

            def add(self, ins):
                self.n += 1
                ins.then_inc(self.done, 1)
                self.eng.wait_ge(self.done, self.n)

        def bc(ap, dims):
            return ap.unsqueeze(2).to_broadcast([ap.shape[0], ap.shape[1], dims])

        block = ctx.enter_context(nc.Block())

        @block.sync
        def _(sp):
            in_v, out_v, ada_v = (w.rearrange("l (k p) f -> l p k f", p=P) for w in (w_in, w_out, w_ada))
            gate_v, up_v, down_v = (w.rearrange("l e (k p) f -> (l e) p k f", p=P) for w in (w_gate, w_up, w_down))

            def load(j, turn, src, at, n):
                sp.wait_ge(slot_free[j], turn * 2 + 1)
                settle(sp)
                sp.dma_start(ring[j][:, :, :], src[bass.ds(at, 1), :, :, 512 * n:512 * n + 512].rearrange("o p k f -> (o p) k f"))\
                    .then_inc(slot_loaded[j], 16)

            with sp.Fori(0, LAYERS) as layer:
                for n in range(ADA // 512):
                    load(n % RING, layer * TURNS + n // RING, ada_v, layer, n)
                turn = layer * TURNS + 2
                for n in range(MIX_CHUNKS):
                    load(n, turn, in_v, layer, n)
                for n in range(2):
                    load(4 + n, turn, out_v, layer, n)
                with sp.Fori(0, EXPERTS) as e:
                    turn = layer * TURNS + e + 3
                    for j, (w, n) in enumerate([(gate_v, 0), (up_v, 0), (gate_v, 1), (up_v, 1), (down_v, 0), (down_v, 1)]):
                        load(j, turn, w, layer * EXPERTS + e, n)

        @block.gpsimd
        def _(pool):
            clear = range(nums[0], nums[-1] + 1)

            def meet(n):
                pool.drain()
                pool.wait_ge(arrived, n * 3)
                settle(pool)
                pool.sem_clear(clear)
                pool.sem_inc(released, 1)

            pool.dma_start(con[:, :], consts[:, :]).then_inc(consts_in, 16)
            pool.dma_start(x_d[:, :], x[:, :]).then_inc(x_out, 16)
            pool.dma_start(nat[0:2, 0:D], c[:, :]).then_inc(consts_in, 16)
            pool.memset(neg_half[:, :], -0.5).then_inc(started, 1)
            pool.wait_ge(started, 1)
            pool.memset(aff[:, :, :, :], 0.0).then_inc(started, 1)
            pool.wait_ge(started, 2)
            pool.wait_ge(x_out, 16)
            pool.wait_ge(consts_in, 32)

            def powers(count):
                def go(n):
                    pool.wait_ge(var_ready, n)
                    pool.tensor_tensor(stat[:, 8:8 + count], stat[:, 0:count], neg_half[:, 0:count], ALU.pow)\
                        .then_inc(rstd_ready, 1)
                return go

            def prepare(layer):
                pad = xn[0:4 * ROW_OFF, 0:128]
                pool.memset(pad, 0.0).then_inc(pad_ready, 1)
                pool.wait_ge(pad_ready, 1)
                pool.dma_start(xn[0:4 * ROW_OFF, 48:48 + COL_OFF],
                               rpb[bass.ds(layer, 1), :, :, :].rearrange("l h r c -> (l h r) c")).then_inc(skew_in, 16)
                b = b_ada[bass.ds(layer, 1), :]
                pool.dma_start(qT[0:2, :, :].rearrange("p a b -> p (a b)"),
                               b[:, 0:4096].to_broadcast([2, 4096])).then_inc(layer_in, 16)
                pool.dma_start(kT[0:2, :, :].rearrange("p a b -> p (a b)"),
                               b[:, 4096:6144].to_broadcast([2, 2048])).then_inc(layer_in, 16)
                pool.dma_start(router[:, :, :],
                               w_router[bass.ds(layer, 1), :, :].rearrange("l (k p) e -> (l p) k e", p=P)).then_inc(layer_in, 16)
                pool.dma_start(sinks[:, :], sink[bass.ds(layer, 1), :].to_broadcast([P, 8])).then_inc(layer_in, 16)
                for h in range(6):
                    g = q_gain if h < 4 else k_gain
                    pool.dma_start(gain_b[:, h, :], g[bass.ds(layer, 1), :].to_broadcast([P, HD])).then_inc(layer_in, 16)
                pool.wait_ge(skew_in, layer * 16 + 16)
                settle(pool)
                pool.dma_start(skew_d[:, :, :], pad.unsqueeze(1).to_broadcast([4 * ROW_OFF, GRID, 128])).then_inc(skew_out, 16)
                pool.wait_ge(skew_out, layer * 16 + 16)
                settle(pool)
                for h in range(4):
                    for r in range(2):
                        src = bass.AP(skew_d.tensor, (h * ROW_OFF + 1 - r) * GRID * 128 + 63,
                                      [[127, GRID], [GRID * 128, 14], [1, GRID]])
                        pool.dma_start(bias_c[r * GRID:(r + 1) * GRID, h, :, :], src).then_inc(bias_in, 16)
                pool.wait_ge(ada_added, 12)
                pool.dma_start(mod_d[:, 0:4096], qT[0:2, :, :].rearrange("p a b -> p (a b)")).then_inc(mod_out, 16)
                pool.dma_start(mod_d[:, 4096:6144], kT[0:2, :, :].rearrange("p a b -> p (a b)")).then_inc(mod_out, 16)
                pool.wait_ge(mod_out, layer * 32 + 32)
                settle(pool)

            def attend(layer, s):
                it = layer * SEQS + s
                rows = s * SEQ
                v0 = hT[0][:, :, :].rearrange("p a b -> p (a b)")
                for n, (src, at, w) in enumerate([(mod_d, 0, 1), (mod_d, D, 1), (mod_d, 3 * D, 1), (mod_d, 4 * D, 1),
                                                  (g_mix, 0, 0), (g_ffn, 0, 0), (g_grp, 0, 0)]):
                    row = src[bass.ds(s if w else layer, 1), at:at + D]
                    pool.dma_start(v0[8 * n:8 * n + 8, 0:P], row.rearrange("o (k p) -> (o k) p", p=P)).then_inc(vec_in, 16)
                pool.dma_start(gate1[:, :], mod_d[bass.ds(s, 1), 2 * D:3 * D].to_broadcast([P, D])).then_inc(vec_in, 16)
                n = 0
                for i in range(TILES + 2):
                    if i < TILES:
                        n += 1
                        powers(1)(n)
                    if i >= 2:
                        n += 1
                        powers(6)(n)
                for kind, i, k in schedule():
                    if kind == "finish":
                        n += 1
                        powers(3)(n)
                    if kind == "norm":
                        n += 1
                        pool.wait_ge(x_new, i + 1)
                        pool.dma_start(x_d[bass.ds(rows + i * P, P), :], X[i][:, :]).then_inc(x_out, 16)
                        powers(1)(n)
                    if kind == "normed_0":
                        pool.wait_ge(xn_new, i + 1)
                        pool.dma_start(xn_d[bass.ds(rows + i * P, P), :], xn[:, :]).then_inc(xn_out, 16)
                        pool.wait_ge(x_out, it * 64 + 16 * i + 32)
                        settle(pool)
                pool.wait_ge(xn_out, it * 64 + 64)
                settle(pool)

            def experts(layer, g):
                it = layer * GROUPS + g
                for j in range(GROUP):
                    pool.wait_ge(idx_ready, 1)
                    pool.indirect_dma_start(out=X[j][:, :], out_offset=None, in_=xn_d[:, :],
                                            in_offset=bass.IndirectOffsetOnAxis(ap=idx_now[j][:, 0:1], axis=0))\
                        .then_inc(gathered[j], 16)
                for j in range(GROUP):
                    pool.wait_ge(y_scaled, 2 * (j + 1))
                    pool.indirect_dma_start(out=x_d[:, :],
                                            out_offset=bass.IndirectOffsetOnAxis(ap=idx_now[j][:, 0:1], axis=0),
                                            in_=xn[:, :] if j % 2 else nat[:, 0:D], in_offset=None,
                                            compute_op=ALU.add).then_inc(scattered, 16)
                    pool.wait_ge(scattered, it * 64 + 16 * j + 16)
                    settle(pool)

            with pool.Fori(0, LAYERS) as layer:
                prepare(layer)
                meet(layer * EPOCHS + 1)
                pool.dma_start(gate2[0:64, :], mod_d[0:1, 5 * D:6 * D].to_broadcast([64, D])).then_inc(gate2_in, 16)
                pool.dma_start(gate2[64:128, :], mod_d[1:2, 5 * D:6 * D].to_broadcast([64, D])).then_inc(gate2_in, 16)
                pool.wait_ge(gate2_in, layer * 32 + 32)
                settle(pool)
                with pool.Fori(0, SEQS) as s:
                    attend(layer, s)
                    meet(layer * EPOCHS + s + 2)
                meet(layer * EPOCHS + 4)
                with pool.Fori(0, GROUPS) as g:
                    experts(layer, g)
                    meet(layer * EPOCHS + g + 5)
            pool.dma_start(gate1[:, :], g_final.rearrange("(a n) -> a n", a=1).to_broadcast([P, D])).then_inc(vec_in, 16)
            for t in range(SEQS * TILES):
                powers(1)(t + 1)
                pool.wait_ge(xn_new, t + 1)
                pool.dma_start(y[t * P:(t + 1) * P, :], X[t % TILES][:, :]).then_inc(y_out, 16)
                pool.wait_ge(y_out, 16 * (t + 1))

        @block.scalar
        def _(act):
            act.wait_ge(started, 2)
            act.wait_ge(consts_in, 32)
            act.activation(nat[0:2, 0:D], nat[0:2, 0:D], ACT.Silu).then_inc(act_done, 1)
            act.wait_ge(vec_turned, 1)
            act.activation(silu_c[:, :, :], bank[0][:, 0:KT * SEQS].rearrange("p (k s) -> p k s", s=SEQS),
                           ACT.Copy).then_inc(xn_ready, 1)

            def attend(layer, s):
                it = layer * SEQS + s
                for i in range(TILES):
                    act.dma_start(X[i][:, :], x_d[bass.ds(s * SEQ + i * P, P), :]).then_inc(x_in[i], 16)

                def normed(i):
                    act.wait_ge(vec_ready, 1)
                    if i >= 2:
                        act.wait_ge(proj_done, 4 * (i - 1))
                    for k in range(KT):
                        if k % 4 == 0:
                            act.wait_ge(h_turned, 2 * i + k // 4 + 1)
                        ins = act.activation(hT[i % 2][:, k, :], bank[k // 4][:, (k % 4) * P:(k % 4 + 1) * P],
                                             ACT.Identity, scale=vec[:, V_SC1 + k:V_SC1 + k + 1],
                                             bias=vec[:, V_SH1 + k:V_SH1 + k + 1])
                        if k % 4 == 3:
                            ins.then_inc(h_ready, 1)

                def copies(i):
                    act.wait_ge(proj_done, 4 * i + 3)
                    if i:
                        act.wait_ge(nat_ready, i)
                    act.activation(pbuf[:, 0, 256:384], bank[4][:, 0:128], ACT.Copy)
                    act.activation(V[:, i, 128:256], bank[4][:, 128:256], ACT.Copy)
                    if i:
                        act.wait_ge(qk_turned, 3 * i)
                    act.activation(nat[:, 768:1024], bank[4][:, 256:512], ACT.Copy).then_inc(proj_read_s, 1)
                    act.wait_ge(proj_done, 4 * i + 4)
                    act.activation(nat[:, 1280:1536], bank[5][:, 0:256], ACT.Copy).then_inc(kc_ready, 1)
                    act.activation(V[:, i, 256:512], bank[5][:, 256:512], ACT.Copy).then_inc(proj_read_s, 1)

                def turned(i):
                    for n in range(3):
                        act.wait_ge(qk_turned, 3 * i + n + 1)
                        dst = qT[:, 4 * n:4 * n + 4, i * P:(i + 1) * P] if n < 2 else kT[:, :, i * P:(i + 1) * P]
                        act.activation(dst, bank[6 + n % 2][:, :].rearrange("p (a b) -> p a b", a=4), ACT.Copy,
                                       scale=-(HD ** -0.5) if n < 2 else 1.0).then_inc(qk_copied, 1)

                normed(0)
                for i in range(TILES):
                    if i + 1 < TILES:
                        normed(i + 1)
                    if i:
                        turned(i - 1)
                    copies(i)
                turned(TILES - 1)

                side = 0
                for kind, i, k in schedule():
                    if kind == "slot":
                        if k < UNITS:
                            u = k % 16
                            grp, *_, st = unit(u)
                            n = keys(i, u)[1] * P
                            act.wait_ge(biased, k + 1)
                            src = bank[k % 3][:, 0:n] if grp == "B" else pbuf[:, k % 3, 0:n]
                            if k >= 3:
                                act.wait_ge(p_turned, k - 2)
                            act.activation(pbuf[:, k % 3, 0:n], src, ACT.Exp, scale=-1.0, bias=smin[:, i % 2, st:st + 1],
                                           accum_out=ssum[:, i % 2, st:st + 1]).then_inc(probs_ready, 1)
                        m = k - T_LAG
                        if 0 <= m < UNITS and m % 2 == 0:
                            n = keys(m // 16, m % 16)[1] * P
                            act.wait_ge(p_turned, m + 1)
                            if m >= 2:
                                act.wait_ge(pv_done, m - 1)
                            act.activation(pbuf[:, 3, 0:n], bank[3][:, 0:n], ACT.Copy).then_inc(pt_by_s, 1)
                    if kind == "finish":
                        act.wait_ge(sink_arg, i + 1)
                        act.activation(stat[:, 16:24], stat[:, 16:24], ACT.Exp).then_inc(sink_exp, 1)
                    if kind in ("normed_0", "normed_1"):
                        half = int(kind[-1])
                        act.wait_ge(side_full, 7 * i + 5 + half)
                        for k4 in range(4):
                            kk = 4 * half + k4
                            ins = act.activation(hT[1][:, kk, :], bank[7][:, k4 * P:(k4 + 1) * P], ACT.Identity,
                                                 scale=vec[:, V_SC2 + kk:V_SC2 + kk + 1],
                                                 bias=vec[:, V_SH2 + kk:V_SH2 + kk + 1])
                        ins.then_inc(side_free, 1)
                    if kind == "router":
                        act.wait_ge(logit_max, i + 1)
                        act.activation(soft[:, 0:EXPERTS], bank[7][:, 0:EXPERTS], ACT.Exp, bias=soft[:, 16:17],
                                       accum_out=soft[:, 17:18]).then_inc(aff_exp, 1)

            def experts():
                def hidden_copy(j, half):
                    act.wait_ge(hid_turned, 2 * j + half + 1)
                    if j >= 1:
                        act.wait_ge(y_done, 2 * j)
                    act.activation(hidT[:, 4 * half:4 * half + 4, :],
                                   bank[4 + half][:, :].rearrange("p (a b) -> p a b", a=4), ACT.Copy).then_inc(hid_copied, 1)

                for j in range(GROUP):
                    for half in range(2):
                        n = 2 * j + half
                        act.wait_ge(gu_done, 2 * n + 1)
                        if n >= 2:
                            act.wait_ge(hid_ready, n - 1)
                        act.activation(pbuf[:, half, :], bank[half][:, :], ACT.Silu).then_inc(silu_done, 1)
                        if half == 1:
                            hidden_copy(j, 0)
                    hidden_copy(j, 1)

            with act.Fori(0, LAYERS) as layer:
                barrier(act, layer * EPOCHS + 1)
                with act.Fori(0, SEQS) as s:
                    attend(layer, s)
                    barrier(act, layer * EPOCHS + s + 2)
                barrier(act, layer * EPOCHS + 4)
                with act.Fori(0, GROUPS) as g:
                    experts()
                    barrier(act, layer * EPOCHS + g + 5)
            for t in range(SEQS * TILES):
                if t >= TILES:
                    act.wait_ge(y_out, 16 * (t - TILES + 1))
                act.dma_start(X[t % TILES][:, :], x_d[t * P:(t + 1) * P, :]).then_inc(x_in[t % TILES], 16)

        @block.vector
        def _(dve):
            def ada(layer):
                chain = Chain(dve, dve_done)
                dve.wait_ge(layer_in, layer * 160 + 160)
                settle(dve)
                chain.add(dve.tensor_scalar(nsink[:, :], sinks[:, :], -1.0, None, ALU.mult))
                dve.wait_ge(bias_in, layer * 128 + 128)
                settle(dve)
                chain.add(dve.scalar_tensor_tensor(
                    out=bias_c[:, :, :, :].rearrange("p h m c -> p (h m) c"),
                    in0=bias_c[:, :, :, :].rearrange("p h m c -> p (h m) c"), scalar=-1.0,
                    in1=mask_c.unsqueeze(1).to_broadcast([P, 56, GRID]), op0=ALU.mult, op1=ALU.add))
                for n in range(12):
                    dve.wait_ge(ada_mm, n + 1)
                    dst = qT[0:2, n, :] if n < 8 else kT[0:2, n - 8, :]
                    dve.tensor_tensor(dst, dst, bank[n % 2][0:2, :], ALU.add).then_inc(ada_added, 1)

            def attend(layer, s):
                it = layer * SEQS + s
                chain = Chain(dve, dve_done)
                rn = [0]

                def rstd(count):
                    rn[0] += 1
                    dve.wait_ge(rstd_ready, rn[0])

                dve.wait_ge(vec_turned, 1)
                chain.add(dve.tensor_copy(vec[:, :], bank[0][:, 0:V_END]))
                for sc, g in ((V_SC1, V_GMIX), (V_SC2, V_GFFN)):
                    ins = dve.scalar_tensor_tensor(out=vec[:, sc:sc + 8], in0=vec[:, sc:sc + 8], scalar=1.0,
                                                   in1=vec[:, g:g + 8], op0=ALU.add, op1=ALU.mult)
                    if sc == V_SC2:
                        ins.then_inc(vec_ready, 1)
                dve.wait_ge(vec_ready, 1)
                chain.add(dve.tensor_copy(mod_e[:, 0, :, bass.ds(s, 1)], vec[:, V_SC2:V_SC2 + 8].unsqueeze(2)))
                chain.add(dve.tensor_copy(mod_e[:, 1, :, bass.ds(s, 1)], vec[:, V_SH2:V_SH2 + 8].unsqueeze(2)))

                def norm(i):
                    dve.wait_ge(x_in[i], it * 16 + 16)
                    if i:
                        dve.wait_ge(h_turned, 2 * i)
                    settle(dve)
                    dve.tensor_tensor_reduce(xn[:, :], X[i][:, :], X[i][:, :], 1.0 / D, EPS, ALU.mult, ALU.add,
                                             stat[:, 0:1]).then_inc(var_ready, 1)
                    rstd(1)
                    dve.tensor_scalar(xn[:, :], X[i][:, :], stat[:, 8:9], None, ALU.mult).then_inc(xn_ready, 1)

                def rotate(dst, src, cs, heads, half, t2):
                    a, b = src.shape[1], src.shape[2]
                    nb = HD // (2 * half)
                    cos = cs[:, 0:HD].unsqueeze(1).to_broadcast([P, b, HD])
                    for q in range(a):
                        chain.add(dve.tensor_tensor(dst[:, q], src[:, q], cos, ALU.mult))
                        for blk in range(nb):
                            o = blk * 2 * half
                            for lo, hi in ((o, o + half), (o + half, o)):
                                sin = cs[:, HD + lo:HD + lo + half].unsqueeze(1).to_broadcast([P, b, half])
                                ins = dve.tensor_tensor(t2[:, q, :, lo:lo + half], src[:, q, :, hi:hi + half], sin, ALU.mult)
                        chain.add(ins)
                        ins = dve.tensor_tensor(dst[:, q], dst[:, q], t2[:, q], ALU.add)
                    return ins

                def rope(i):
                    r0 = C_ROPE + 256 * i
                    ca, cb = con[:, r0:r0 + 128], con[:, r0 + 128:r0 + 256]
                    flat = pbuf[:, :, :].rearrange("p a b -> p (a b)")
                    t2 = flat[:, 512:1024].rearrange("p (a b d) -> p a b d", a=2, d=HD)
                    dve.wait_ge(proj_done, 4 * i + 1)
                    if i:
                        dve.wait_ge(qk_turned, 3 * i)
                    chain.add(rotate(nat[:, 0:512].rearrange("p (j g d) -> p g j d", j=4, g=2),
                                     bank[2][:, :].rearrange("p (g j d) -> p g j d", g=2, j=4), ca, 8, 32, t2))
                    dve.sem_inc(proj_read_v, 1)
                    dve.wait_ge(proj_done, 4 * i + 2)
                    chain.add(rotate(nat[:, 1024:1152].rearrange("p (a b d) -> p a b d", a=1, d=HD),
                                     bank[3][:, 0:128].rearrange("p (a b d) -> p a b d", a=1, d=HD), ca, 2, 32,
                                     flat[:, 512:640].rearrange("p (a b d) -> p a b d", a=1, d=HD)))
                    xb = flat[:, 0:384]
                    dve.tensor_copy(V[:, i, 0:128], bank[3][:, 128:256])
                    dve.tensor_copy(xb[:, 0:256], bank[3][:, 256:512]).then_inc(proj_read_v, 1)
                    dve.wait_ge(proj_read_v, 2 * i + 2)
                    dve.wait_ge(proj_read_s, 2 * i + 1)
                    sq = flat[:, 512:896]
                    xb3 = xb.rearrange("p (h d) -> p h d", d=HD)
                    chain.add(dve.tensor_tensor(sq, xb, xb, ALU.mult))
                    chain.add(dve.tensor_reduce(stat[:, 24:30], sq.rearrange("p (h d) -> p h d", d=HD), AX.X, ALU.add))
                    dve.tensor_scalar(stat[:, 0:6], stat[:, 24:30], 1.0 / HD, EPS, ALU.mult, ALU.add).then_inc(var_ready, 1)
                    rstd(6)
                    chain.add(dve.tensor_tensor(xb3, xb3, bc(stat[:, 8:14], HD), ALU.mult))
                    chain.add(dve.tensor_tensor(xb3, xb3, gain_b[:, :, :], ALU.mult))
                    chain.add(rotate(nat[:, 512:768].rearrange("p (j g d) -> p g j d", j=2, g=2),
                                     xb[:, 0:256].rearrange("p (g j d) -> p g j d", g=2, j=2), cb, 4, 16,
                                     flat[:, 512:768].rearrange("p (a b d) -> p a b d", a=2, d=HD)))
                    rotate(nat[:, 1152:1280].rearrange("p (a b d) -> p a b d", a=1, d=HD),
                           xb[:, 256:384].rearrange("p (a b d) -> p a b d", a=1, d=HD), cb, 2, 16,
                           flat[:, 512:640].rearrange("p (a b d) -> p a b d", a=1, d=HD)).then_inc(nat_ready, 1)

                norm(0)
                norm(1)
                for i in range(TILES):
                    if i + 2 < TILES:
                        norm(i + 2)
                    rope(i)

                def ttr_min(out, in0, in1, first, acc):
                    return dve.tensor_tensor_reduce(out, in0, in1, 1.0, first, ALU.add, ALU.min, acc)

                for kind, i, k in schedule():
                    if kind == "slot":
                        if k < UNITS:
                            u = k % 16
                            grp, *_, st = unit(u)
                            lo, nb = keys(i, u)
                            dve.wait_ge(scored, k + 1)
                            if k >= 3:
                                dve.wait_ge(p_turned, k - 2)
                            src, dst, acc = bank[k % 3][:, 0:nb * P], pbuf[:, k % 3, 0:nb * P], smin[:, i % 2, st:st + 1]
                            if grp == "A":
                                off = (lo - (i - 1)) * P
                                ins = ttr_min(dst, src, mask_a[:, off:off + nb * P], nsink[:, st:st + 1], acc)
                            elif grp == "B":
                                ins = dve.tensor_reduce(acc, src, AX.X, ALU.min)
                            else:
                                m = 7 - 2 * i - 1
                                ins = ttr_min(dst, src, bias_c[:, st - 12, m:m + NA_ROWS, :].rearrange("p m c -> p (m c)"),
                                              3e38, acc)
                            ins.then_inc(biased, 1)
                        m = k - T_LAG
                        if 0 <= m < UNITS and m % 2 == 1:
                            n = keys(m // 16, m % 16)[1] * P
                            dve.wait_ge(p_turned, m + 1)
                            if m >= 2:
                                dve.wait_ge(pv_done, m - 1)
                            dve.tensor_copy(pbuf[:, 4, 0:n], bank[4][:, 0:n]).then_inc(pt_by_v, 1)
                    if kind == "finish":
                        dve.wait_ge(probs_ready, 16 * (i + 1))
                        dve.tensor_tensor(stat[:, 16:24], smin[:, i % 2, 0:8], sinks[:, :], ALU.add).then_inc(sink_arg, 1)
                        dve.wait_ge(sink_exp, i + 1)
                        chain.add(dve.tensor_tensor(ssum[:, i % 2, 0:8], ssum[:, i % 2, 0:8], stat[:, 16:24], ALU.add))
                        chain.add(dve.reciprocal(rinv[:, :], ssum[:, i % 2, :]))
                        dve.wait_ge(pv_done, 16 * (i + 1))
                        if i:
                            dve.wait_ge(side_full, 7 * (i - 1) + 2)
                        og3 = og.rearrange("p (h d) -> p h d", d=HD)
                        for half in range(2):
                            ins = dve.tensor_tensor(og3[:, 8 * half:8 * half + 8, :],
                                                    bank[5 + half][:, :].rearrange("p (h d) -> p h d", d=HD),
                                                    bc(rinv[:, 8 * half:8 * half + 8], HD), ALU.mult)
                        ins.then_inc(heads_read, 1)
                        dve.wait_ge(heads_read, i + 1)
                        if i:
                            dve.wait_ge(side_full, 7 * (i - 1) + 4)
                        junk = hT[0][:, :, :].rearrange("p a b -> p (a b)")
                        groups = ((0, 512), (512, 256), (768, 256))
                        for n, (o, w) in enumerate(groups):
                            ins = dve.tensor_tensor_reduce(junk[:, o:o + w], og[:, o:o + w], og[:, o:o + w], 1.0 / w, EPS,
                                                           ALU.mult, ALU.add, stat[:, n:n + 1])
                        ins.then_inc(var_ready, 1)
                        rstd(3)
                        for n, (o, w) in enumerate(groups):
                            ins = dve.tensor_scalar(og[:, o:o + w], og[:, o:o + w], stat[:, 8 + n:9 + n], None, ALU.mult)
                        ins.then_inc(merged, 1)
                    if kind in ("merged_0", "merged_1"):
                        half = int(kind[-1])
                        dve.wait_ge(side_full, 7 * i + 1 + half)
                        dve.tensor_tensor(hT[0][:, 4 * half:4 * half + 4, :], bank[7][:, :].rearrange("p (a b) -> p a b", a=4),
                                          bc(vec[:, V_GGRP + 4 * half:V_GGRP + 4 * half + 4], P), ALU.mult)\
                            .then_inc(side_free, 1)
                    if kind in ("out_0", "out_1"):
                        half = int(kind[-1])
                        cols = slice(512 * half, 512 * half + 512)
                        dve.wait_ge(side_full, 7 * i + 3 + half)
                        if i and not half:
                            dve.wait_ge(xn_out, it * 64 + 16 * i)
                            settle(dve)
                        dve.tensor_tensor(xn[:, cols], bank[7][:, :], gate1[:, cols], ALU.mult).then_inc(side_free, 1)
                        dve.wait_ge(side_free, 7 * i + 3 + half)
                        chain.add(dve.tensor_tensor(X[i][:, cols], X[i][:, cols], xn[:, cols], ALU.add))
                        if half:
                            dve.sem_inc(x_new, 1)
                    if kind == "norm":
                        dve.tensor_tensor_reduce(xn[:, :], X[i][:, :], X[i][:, :], 1.0 / D, EPS, ALU.mult, ALU.add,
                                                 stat[:, 0:1]).then_inc(var_ready, 1)
                        rstd(1)
                        dve.tensor_scalar(xn[:, :], X[i][:, :], stat[:, 8:9], None, ALU.mult).then_inc(xn_new, 1)
                    if kind == "router":
                        dve.wait_ge(side_full, 7 * i + 7)
                        dve.tensor_reduce(soft[:, 16:17], bank[7][:, 0:EXPERTS], AX.X, ALU.max, negate=True).then_inc(logit_max, 1)
                        dve.wait_ge(aff_exp, i + 1)
                        chain.add(dve.reciprocal(soft[:, 18:19], soft[:, 17:18]))
                        dve.tensor_scalar(aff[:, i, bass.ds(s, 1), 0:EXPERTS].rearrange("p o e -> p (o e)"),
                                          soft[:, 0:EXPERTS], soft[:, 18:19], None, ALU.mult).then_inc(side_free, 1)

            def route():
                chain = Chain(dve, dve_done)
                dve.wait_ge(route_turned, 1)
                scores = hT[0][0:64, 0:4, :].rearrange("p a b -> p (a b)")
                sel = xn[0:64, 0:2 * CAP]
                found = pbuf[0:64, 0, 0:CAP].bitcast(u32)
                chain.add(dve.tensor_copy(scores, bank[0][0:64, :]))
                for r in range(CAP // 8):
                    top = sel[:, CAP + 8 * r:CAP + 8 * r + 8]
                    chain.add(dve.max(top, scores))
                    chain.add(dve.max_index(found[:, 8 * r:8 * r + 8], top, scores))
                    chain.add(dve.match_replace(out=scores, in_to_replace=top, in_values=scores, imm_value=-1.0))
                dve.tensor_copy(sel[:, 0:CAP], found).then_inc(route_ready, 1)
                dve.wait_ge(route_turned, 2)
                b = bank[1]
                dve.tensor_copy(idx_f[0:64, :], b[0:64, 0:16])
                dve.tensor_scalar(idx_f[64:128, :], b[0:64, 32:48], float(SEQ), None, ALU.add)
                dve.tensor_copy(gate_t[0:64, :], b[64:128, 0:16])
                chain.add(dve.tensor_copy(gate_t[64:128, :], b[64:128, 32:48]))
                chain.add(dve.tensor_copy(idx_t[:, :], idx_f[:, :]))

            def experts(layer, g):
                chain = Chain(dve, dve_done)
                it = layer * GROUPS + g
                for j in range(GROUP):
                    ins = dve.tensor_copy(idx_now[j][:, 0:1], idx_t[:, bass.ds(g * GROUP + j, 1)])
                ins.then_inc(idx_ready, 1)
                chain.add(dve.tensor_copy(gate_now[:, :], gate_t[:, bass.ds(g * GROUP, GROUP)]))

                def modulate(j):
                    for half in range(2):
                        dve.wait_ge(xe_turned, 2 * j + half + 1)
                        if j >= 2:
                            dve.wait_ge(gu_done, 4 * (j - 1))
                        dst = hT[j % 2][:, 4 * half:4 * half + 4, :].rearrange("p k (s t) -> p (k s) t", s=SEQS)
                        a = mod_e[:, 0, 4 * half:4 * half + 4, :].rearrange("p k s -> p (k s)")
                        b = mod_e[:, 1, 4 * half:4 * half + 4, :].rearrange("p k s -> p (k s)")
                        chain.add(dve.tensor_tensor(dst, bank[4 + (half + (j > 0)) % 2][:, :].rearrange("p (a b) -> p a b", a=8),
                                                    bc(a, 64), ALU.mult))
                        dve.tensor_tensor(dst, dst, bc(b, 64), ALU.add).then_inc(xe_ready, 1)

                def scale_out(j):
                    dst = xn if j % 2 else nat
                    for half in range(2):
                        dve.wait_ge(y_done, 2 * j + half + 1)
                        if j >= 2:
                            dve.wait_ge(scattered, it * 64 + 16 * (j - 1))
                            settle(dve)
                        dve.scalar_tensor_tensor(out=dst[:, 512 * half:512 * half + 512], in0=bank[6 + half][:, :],
                                                 scalar=gate_now[:, j:j + 1], in1=gate2[:, 512 * half:512 * half + 512],
                                                 op0=ALU.mult, op1=ALU.mult).then_inc(y_scaled, 1)

                modulate(0)
                for j in range(GROUP):
                    for half in range(2):
                        n = 2 * j + half
                        dve.wait_ge(silu_done, n + 1)
                        dve.wait_ge(gu_done, 2 * n + 2)
                        if n >= 2:
                            dve.wait_ge(hid_turned, n - 1)
                        dve.tensor_tensor(pbuf[:, 2 + half, :], pbuf[:, half, :], bank[2 + half][:, :], ALU.mult)\
                            .then_inc(hid_ready, 1)
                        if half == 0 and j:
                            scale_out(j - 1)
                    if j + 1 < GROUP:
                        modulate(j + 1)
                scale_out(GROUP - 1)

            with dve.Fori(0, LAYERS) as layer:
                ada(layer)
                barrier(dve, layer * EPOCHS + 1)
                with dve.Fori(0, SEQS) as s:
                    attend(layer, s)
                    barrier(dve, layer * EPOCHS + s + 2)
                route()
                barrier(dve, layer * EPOCHS + 4)
                with dve.Fori(0, GROUPS) as g:
                    experts(layer, g)
                    barrier(dve, layer * EPOCHS + g + 5)
            dve.wait_ge(vec_in, 16 * (8 * LAYERS * SEQS + 1))
            for t in range(SEQS * TILES):
                dve.wait_ge(x_in[t % TILES], 16 * (LAYERS * SEQS + t // TILES + 1))
                xt = X[t % TILES]
                dve.tensor_tensor_reduce(xn[:, :], xt[:, :], xt[:, :], 1.0 / D, EPS, ALU.mult, ALU.add,
                                         stat[:, 0:1]).then_inc(var_ready, 1)
                dve.wait_ge(rstd_ready, t + 1)
                dve.scalar_tensor_tensor(out=xt[:, :], in0=xt[:, :], scalar=stat[:, 8:9], in1=gate1[:, :],
                                         op0=ALU.mult, op1=ALU.mult).then_inc(xn_new, 1)

        @block.tensor
        def _(pe):
            for j in range(RING):
                pe.sem_inc(slot_free[j], 1)
            pe.wait_ge(started, 2)
            pe.wait_ge(act_done, 1)
            for k in range(KT):
                ins = pe.transpose(bank[0][:, SEQS * k:SEQS * (k + 1)], nat[0:2, k * P:(k + 1) * P], ident[0:2, 0:2])
            ins.then_inc(vec_turned, 1)
            pe.wait_ge(xn_ready, 1)

            def use(j, turn):
                pe.wait_ge(slot_loaded[j], turn * 16 + 16)
                settle(pe)

            def ada(layer):
                for n in range(12):
                    use(n % RING, layer * TURNS + n // RING)
                    if n >= 2:
                        pe.wait_ge(ada_added, n - 1)
                    for k in range(KT):
                        ins = pe.matmul(bank[n % 2][0:2, :], silu_c[:, k, :], ring[n % RING][:, k, :],
                                        start=(k == 0), stop=(k == KT - 1))
                    ins.then_inc(ada_mm, 1)
                    if n:
                        pe.wait_ge(ada_mm, n)
                        pe.sem_inc(slot_free[(n - 1) % RING], 2)
                pe.wait_ge(ada_mm, 12)
                pe.sem_inc(slot_free[RING - 1], 2)

            def attend(layer, s):
                it = layer * SEQS + s
                turn = layer * TURNS + 2
                v0 = hT[0][:, :, :].rearrange("p a b -> p (a b)")
                pe.wait_ge(vec_in, it * 128 + 128)
                settle(pe)
                pe.transpose(bank[0][:, 0:V_END], v0[0:V_END, 0:P], ident[0:V_END, 0:V_END]).then_inc(vec_turned, 1)
                pe.wait_ge(vec_ready, 1)

                def turn_h(i):
                    pe.wait_ge(xn_ready, i + 1)
                    for k in range(KT):
                        if k % 4 == 0 and i:
                            pe.wait_ge(h_ready, 2 * i - 1 + k // 4)
                        ins = pe.transpose(bank[k // 4][:, (k % 4) * P:(k % 4 + 1) * P], xn[:, k * P:(k + 1) * P], ident)
                        if k % 4 == 3:
                            ins.then_inc(h_turned, 1)

                def turn_qk(i):
                    pe.wait_ge(nat_ready, i + 1)
                    pe.wait_ge(kc_ready, i + 1)
                    for n in range(3):
                        if 3 * i + n >= 2:
                            pe.wait_ge(qk_copied, 3 * i + n - 1)
                        if n == 0 and i:
                            pe.wait_ge(qk_copied, 3 * i)
                        for a in range(4):
                            o = 512 * n + P * a
                            ins = pe.transpose(bank[6 + n % 2][:, a * P:(a + 1) * P], nat[:, o:o + P], ident)
                        ins.then_inc(qk_turned, 1)

                turn_h(0)
                for i in range(TILES):
                    if i + 1 < TILES:
                        turn_h(i + 1)
                    pe.wait_ge(h_ready, 2 * i + 2)
                    for ch in range(MIX_CHUNKS):
                        if i == 0:
                            use(ch, turn)
                        else:
                            pe.wait_ge(proj_read_v if ch < 2 else proj_read_s, 2 * (i - 1) + ch % 2 + 1)
                        for k in range(KT):
                            ins = pe.matmul(bank[2 + ch][:, :], hT[i % 2][:, k, :], ring[ch][:, k, :],
                                            start=(k == 0), stop=(k == KT - 1))
                        ins.then_inc(proj_done, 1)
                        if i and ch == 1:
                            turn_qk(i - 1)
                pe.wait_ge(proj_done, 4 * TILES)
                for ch in range(MIX_CHUNKS):
                    pe.sem_inc(slot_free[ch], 1)
                turn_qk(TILES - 1)
                pe.wait_ge(proj_read_v, 2 * TILES)
                pe.wait_ge(proj_read_s, 2 * TILES)
                pe.wait_ge(qk_copied, 3 * TILES)
                use(4, turn)
                use(5, turn)

                side = 0

                def side_turn(i):
                    if side:
                        pe.wait_ge(side_free, side)

                for kind, i, k in schedule():
                    if kind == "slot":
                        if k < UNITS:
                            grp, qp, g, kp, _, _, _ = unit(k % 16)
                            lo, nb = keys(i, k % 16)
                            if k >= 3:
                                pe.wait_ge(probs_ready, k - 2)
                            rows = slice(HD * g, HD * g + HD)
                            pe.matmul(bank[k % 3][:, 0:nb * P], qT[rows, qp, i * P:(i + 1) * P],
                                      kT[rows, kp, lo * P:(lo + nb) * P], start=True, stop=True).then_inc(scored, 1)
                        m = k - T_LAG
                        if 0 <= m < UNITS:
                            nb = keys(m // 16, m % 16)[1]
                            pe.wait_ge(probs_ready, m + 1)
                            if m >= 2:
                                pe.wait_ge(pt_by_v if m % 2 else pt_by_s, m // 2)
                            for b in range(nb):
                                ins = pe.transpose(bank[3 + m % 2][:, b * P:(b + 1) * P], pbuf[:, m % 3, b * P:(b + 1) * P], ident)
                            ins.then_inc(p_turned, 1)
                        m = k - V_LAG
                        if 0 <= m < UNITS:
                            _, _, _, _, vc, oc, _ = unit(m % 16)
                            lo, nb = keys(m // 16, m % 16)
                            pe.wait_ge(pt_by_v if m % 2 else pt_by_s, m // 2 + 1)
                            if m % 16 == 0 and m:
                                pe.wait_ge(heads_read, m // 16)
                            for b in range(nb):
                                ins = pe.matmul(bank[5 + oc // 512][:, oc % 512:oc % 512 + HD],
                                                pbuf[:, 3 + m % 2, b * P:(b + 1) * P], V[:, lo + b, vc:vc + HD],
                                                start=(b == 0), stop=(b == nb - 1))
                            ins.then_inc(pv_done, 1)
                    if kind in ("merged_0", "merged_1"):
                        half = int(kind[-1])
                        side_turn(i)
                        pe.wait_ge(merged, i + 1)
                        for a in range(4):
                            o = 512 * half + P * a
                            ins = pe.transpose(bank[7][:, a * P:(a + 1) * P], og[:, o:o + P], ident)
                        ins.then_inc(side_full, 1)
                        side += 1
                    if kind in ("out_0", "out_1"):
                        half = int(kind[-1])
                        side_turn(i)
                        for kk in range(KT):
                            ins = pe.matmul(bank[7][:, :], hT[0][:, kk, :], ring[4 + half][:, kk, :],
                                            start=(kk == 0), stop=(kk == KT - 1))
                        ins.then_inc(side_full, 1)
                        side += 1
                    if kind in ("normed_0", "normed_1"):
                        half = int(kind[-1])
                        side_turn(i)
                        pe.wait_ge(xn_new, i + 1)
                        for a in range(4):
                            o = 512 * half + P * a
                            ins = pe.transpose(bank[7][:, a * P:(a + 1) * P], xn[:, o:o + P], ident)
                        ins.then_inc(side_full, 1)
                        side += 1
                    if kind == "router":
                        side_turn(i)
                        for kk in range(KT):
                            ins = pe.matmul(bank[7][:, 0:EXPERTS], hT[1][:, kk, :], router[:, kk, :],
                                            start=(kk == 0), stop=(kk == KT - 1))
                        ins.then_inc(side_full, 1)
                        side += 1
                pe.wait_ge(side_full, side)
                pe.sem_inc(slot_free[4], 1)
                pe.sem_inc(slot_free[5], 1)

            def route():
                for t in range(TILES):
                    ins = pe.transpose(bank[0][0:64, t * P:(t + 1) * P], aff[:, t, :, :].rearrange("p s e -> p (s e)"), ident)
                ins.then_inc(route_turned, 1)
                pe.wait_ge(route_ready, 1)
                pe.transpose(bank[1][:, 0:64], xn[0:64, 0:2 * CAP], ident[0:64, 0:64]).then_inc(route_turned, 1)

            def experts(layer, g):
                it = layer * GROUPS + g

                def turn_xe(j, half):
                    if half == 0:
                        pe.wait_ge(gathered[j], it * 16 + 16)
                        settle(pe)
                    if j:
                        if half == 0:
                            if j >= 2:
                                pe.wait_ge(hid_copied, 2 * (j - 1))
                            else:
                                pe.wait_ge(xe_ready, 2)
                        else:
                            pe.wait_ge(hid_copied, 2 * j - 1)
                    for a in range(4):
                        o = 512 * half + P * a
                        ins = pe.transpose(bank[4 + (half + (j > 0)) % 2][:, a * P:(a + 1) * P], X[j][:, o:o + P], ident)
                    ins.then_inc(xe_turned, 1)

                def turn_hid(j, half):
                    pe.wait_ge(hid_ready, 2 * j + half + 1)
                    if half == 0:
                        pe.wait_ge(xe_ready, 2 * j + 2)
                    elif j + 1 < GROUP:
                        pe.wait_ge(xe_ready, 2 * j + 3)
                    if half == 1 and j + 1 == GROUP:
                        pe.wait_ge(hid_copied, 2 * j)
                    for a in range(4):
                        ins = pe.transpose(bank[4 + half][:, a * P:(a + 1) * P], pbuf[:, 2 + half, a * P:(a + 1) * P], ident)
                    ins.then_inc(hid_turned, 1)

                turn_xe(0, 0)
                turn_xe(0, 1)
                for j in range(GROUP):
                    turn = layer * TURNS + g * GROUP + (j + 3)
                    pe.wait_ge(xe_ready, 2 * j + 2)
                    for n in range(4):
                        half = n // 2
                        use(n, turn)
                        if j:
                            pe.wait_ge(hid_ready, 2 * (j - 1) + half + 1)
                        for k in range(KT):
                            ins = pe.matmul(bank[2 * (n % 2) + half][:, :], hT[j % 2][:, k, :], ring[n][:, k, :],
                                            start=(k == 0), stop=(k == KT - 1))
                        ins.then_inc(gu_done, 1)
                        if n:
                            pe.wait_ge(gu_done, 4 * j + n)
                            pe.sem_inc(slot_free[n - 1], 2)
                        elif j:
                            pe.wait_ge(y_done, 2 * j)
                            pe.sem_inc(slot_free[4], 2)
                            pe.sem_inc(slot_free[5], 2)
                    turn_hid(j, 0)
                    if j + 1 < GROUP:
                        turn_xe(j + 1, 0)
                        turn_xe(j + 1, 1)
                    use(4, turn)
                    use(5, turn)
                    if j:
                        pe.wait_ge(y_scaled, 2 * j)
                    pe.wait_ge(hid_copied, 2 * j + 1)
                    for part_k in range(2):
                        if part_k:
                            turn_hid(j, 1)
                            pe.wait_ge(hid_copied, 2 * j + 2)
                        for half in range(2):
                            for k in range(4 * part_k, 4 * part_k + 4):
                                ins = pe.matmul(bank[6 + half][:, :], hidT[:, k, :], ring[4 + half][:, k, :],
                                                start=(k == 0), stop=(k == KT - 1))
                            if part_k:
                                ins.then_inc(y_done, 1)
                            elif half == 0:
                                pe.wait_ge(gu_done, 4 * j + 4)
                                pe.sem_inc(slot_free[3], 2)
                pe.wait_ge(y_done, 2 * GROUP)
                pe.sem_inc(slot_free[4], 2)
                pe.sem_inc(slot_free[5], 2)

            with pe.Fori(0, LAYERS) as layer:
                ada(layer)
                barrier(pe, layer * EPOCHS + 1)
                with pe.Fori(0, SEQS) as s:
                    attend(layer, s)
                    barrier(pe, layer * EPOCHS + s + 2)
                route()
                barrier(pe, layer * EPOCHS + 4)
                with pe.Fori(0, GROUPS) as g:
                    experts(layer, g)
                    barrier(pe, layer * EPOCHS + g + 5)


def constants():
    import numpy as np
    f = np.float32
    out = np.zeros((P, C_END), f)
    out[:, C_ID:C_ID + P] = np.eye(P, dtype=f)
    q, k = np.arange(P)[:, None], np.arange(P)[None, :]
    out[:, C_MASKA:C_MASKA + P] = np.where(k >= q, 0, BIG)
    out[:, C_MASKA + 2 * P:C_MASKA + 3 * P] = np.where(k <= q, 0, BIG)
    col = np.arange(P)[:, None] % GRID
    start = np.clip(col - 8, 0, GRID - 16)
    kc = np.arange(GRID)[None, :]
    out[:, C_MASKC:C_MASKC + GRID] = np.where((kc >= start) & (kc < start + 16), 0, BIG)

    def table(pos, dim):
        inv = f(10000.0) ** (-np.arange(0, dim, 2, dtype=f) / f(dim))
        ang = pos.astype(f)[:, None] * inv[None, :].astype(f)
        return np.concatenate([np.cos(ang)] * 2, 1), np.concatenate([-np.sin(ang), np.sin(ang)], 1)

    t = np.arange(SEQ)
    ca, sa = table(t, HD)
    cr, sr = table(t // GRID, HD // 2)
    cc, sc = table(t % GRID, HD // 2)
    rope = np.concatenate([ca, sa, cr, cc, sr, sc], 1).astype(f)
    for i in range(TILES):
        out[:, C_ROPE + 256 * i:C_ROPE + 256 * (i + 1)] = rope[i * P:(i + 1) * P]
    return out


_NAMES = ["w_ada", "b_ada", "g_mix", "w_in", "sink", "q_gain", "k_gain", "rpb", "g_grp", "w_out", "g_ffn", "w_router",
          "w_gate", "w_up", "w_down", "g_final"]


def kernel(**inputs):
    import numpy as np
    import concourse.bacc as _bacc
    from concourse.bass_utils import run_bass_kernel_spmd as _run

    nc = _bacc.Bacc("TRN2", target_bir_lowering=False, num_devices=1)
    data = {
        "x": np.concatenate([np.asarray(inputs["x_prompt"]).reshape(SEQ, D), np.asarray(inputs["x_sample"]).reshape(SEQ, D)]),
        "c": np.concatenate([np.asarray(inputs["c_prompt"]), np.asarray(inputs["c_sample"])]),
    }
    for name in _NAMES:
        data[name] = np.ascontiguousarray(inputs[name])
    data["consts"] = constants()
    arrays, args = {}, []
    for name, a in data.items():
        arrays[f"in_{name}"] = a
        args.append(nc.dram_tensor(f"in_{name}", a.shape, mybir.dt.from_np(a.dtype), kind="ExternalInput").ap())
    args.append(nc.dram_tensor("out_y", (SEQS * SEQ, D), mybir.dt.float32, kind="ExternalOutput").ap())
    trunk(nc, *args)
    got = _run(nc, [arrays], core_ids=[0]).results[0]["out_y"]
    return got[0:SEQ].reshape(1, SEQ, D), got[SEQ:].reshape(1, SEQ, D)
```

```python
import concourse.bass as bass
from concourse import mybir
from contextlib import ExitStack

LAYERS, SEQS, SEQ, D = 2, 2, 512, 1024
HD = 64
P = 128
KT = D // P
TILES = SEQ // P
MIX_CHUNKS = 4
ADA = 6 * D
EXPERTS, CAP = 16, 64
GROUP = 4
GROUPS = EXPERTS // GROUP
RING = 6
GRID, NA_ROWS, ROW_OFF, COL_OFF = 64, 8, 15, 31
TURNS = ADA // 512 // RING + 1 + EXPERTS
EPOCHS = 1 + SEQS + 1 + 1
AHEAD = 8
EPS = 1e-6
GROUP_COLS = ((0, 512), (512, 256), (768, 256))
BIG = 1e30
UNITS = 16 * TILES
T_LAG, V_LAG = 2, 3

C_ID, C_MASKA, C_MASKC, C_ROPE, C_END = 0, 128, 512, 576, 1600
M_SH1, M_SC1, M_GT1, M_SH2, M_SC2, M_GT2, M_END = 0, 8, 16, 24, 32, 40, 48
R_BIAS, R_GMIX, R_GFFN, R_GGRP, R_END = 0, 48, 56, 64, 72


def unit(u):
    if u < 8:
        j, g = u // 2, u % 2
        h = 4 * g + j
        return "A", j, g, 0, g * HD, h * HD, h
    if u < 12:
        j, g = (u - 8) // 2, u % 2
        h = 2 * g + j
        return "B", 4 + j, g, 1, 128 + g * HD, 512 + h * HD, 8 + h
    j, g = (u - 12) // 2, u % 2
    h = 2 * j + g
    return "C", 6 + j, g, 2 + j, 256 + h * HD, 768 + h * HD, 12 + h


def keys(i, u):
    if u < 8:
        lo, hi = max(i - 1, 0), min(i + 1, TILES - 1)
        return lo, hi - lo + 1
    return 0, TILES


AFTER = [(8, "sink"), (8 + V_LAG, "heads_a"), (9 + V_LAG, "scale_a"), (15 + V_LAG, "heads_b"), (17 + V_LAG, "scale_b"),
         (21, "merged_0"), (22, "merged_1")]
AFTER += [(23 + 4 * half + quarter, f"out_{half}{quarter}") for half in range(2) for quarter in range(4)]
AFTER += [(31, "norm"), (32, "normed"), (33, "normed_0"), (34, "normed_1"), (35, "router_0"), (36, "router_1")]
SLOTS = 16 * (TILES - 1) + AFTER[-1][0] + 1


def schedule():
    out = []
    for k in range(SLOTS):
        out.append(("slot", k // 16, k))
        for i in range(TILES):
            out += [(name, i, k) for at, name in AFTER if 16 * i + at == k]
    return out


def trunk(nc, x, c, w_ada, b_ada, g_mix, w_in, sink, q_gain, k_gain, rpb, g_grp, w_out, g_ffn, w_router,
          w_gate, w_up, w_down, g_final, consts, y):
    f32, u32 = mybir.dt.float32, mybir.dt.uint32
    ALU, ACT, AX = mybir.AluOpType, mybir.ActivationFunctionType, mybir.AxisListType
    ctx = ExitStack()
    with ctx:
        def sb(name, shape, dt=f32):
            return ctx.enter_context(nc.sbuf_tensor(name, shape, dt))

        def sem(name):
            return ctx.enter_context(nc.semaphore(name))

        x_d = nc.dram_tensor("residual", [SEQS * SEQ, D], f32).ap()
        xn_d = nc.dram_tensor("normed", [SEQS * SEQ, D], f32).ap()
        skew_d = nc.dram_tensor("bias_rows", [4 * ROW_OFF, GRID, 128], f32).ap()

        ring = [sb(f"ring{j}", [P, KT, 512]) for j in range(RING)]
        con = sb("con", [P, C_END])
        ident = con[:, C_ID:C_ID + P]
        mask_a = con[:, C_MASKA:C_MASKA + 3 * P]
        mask_c = con[:, C_MASKC:C_MASKC + GRID]
        silu_c = sb("silu_c", [P, KT, SEQS])
        rows_t = sb("rows_t", [P, R_END])
        mods = sb("mods", [P, M_END, SEQS])
        vec = sb("vec", [P, M_END])
        gate1 = sb("gate1", [P, D])
        gate2 = sb("gate2", [P, D])
        bias_c = sb("bias_c", [P, 4, 14, GRID])
        router = sb("router_w", [P, KT, EXPERTS])
        gain_b = sb("gain_b", [P, 6, HD])
        nsink = sb("nsink", [P, 8])
        sinks = sb("sinks", [P, 8])
        neg_half = sb("neg_half", [P, 8])
        aff = sb("aff", [P, TILES, SEQS, 32])
        qT = sb("qT", [P, 8, SEQ])
        kT = sb("kT", [P, 4, SEQ])
        V = sb("V", [P, TILES, 512])
        X = [sb(f"X{i}", [P, D]) for i in range(TILES)]
        xn = sb("xn", [P, D])
        hT = [sb(f"hT{i}", [P, KT, P]) for i in range(2)]
        nat = sb("nat", [P, 1536])
        og = nat[:, 0:D]
        pbuf = sb("pbuf", [P, 5, 512])
        stat = sb("stat", [P, 32])
        smin = sb("smin", [P, 2, 16])
        ssum = sb("ssum", [P, 2, 16])
        rinv = sb("rinv", [P, 16])
        soft = sb("soft", [P, 2, TILES * SEQS])
        hidT = kT[:, 0:2, :].rearrange("p a (b t) -> p (a b) t", t=P)
        idx_t = sb("idx_t", [P, EXPERTS + GROUP], u32)
        idx_f = sb("idx_f", [P, EXPERTS])
        gate_t = sb("gate_t", [P, EXPERTS])
        idx_in = [sb(f"idx_in{j}", [P, 1], u32) for j in range(GROUP)]
        idx_out = [sb(f"idx_out{j}", [P, 1], u32) for j in range(GROUP)]
        gate_now = sb("gate_now", [P, GROUP])
        probs_r = pbuf[:, 4, 0:TILES * SEQS * EXPERTS].rearrange("p (t e) -> p t e", e=EXPERTS)
        bank = [ctx.enter_context(nc.psum_tensor(f"bank{i}", [P, 512], f32)) for i in range(8)]

        slot_loaded = [sem(f"slot_loaded{j}") for j in range(RING)]
        slot_free = [sem(f"slot_free{j}") for j in range(RING)]
        c_turned = sem("c_turned")
        started = sem("started")
        consts_in, passed = sem("consts_in"), sem("passed")
        arrived, released = sem("arrived"), sem("released")
        layer_in = sem("layer_in")
        skew_in, skew_out, bias_in = sem("skew_in"), sem("skew_out"), sem("bias_in")
        rows_in = sem("rows_in")
        final_in = sem("final_in")
        x_in = [sem(f"x_in{i}") for i in range(TILES)]
        x_out, xn_out = sem("x_out"), sem("xn_out")
        x_there = sem("x_there")
        gathered = [sem(f"gathered{j}") for j in range(GROUP)]
        scattered = sem("scattered")
        y_out = sem("y_out")

        cleared = []

        def part(name):
            cleared.append(sem(name))
            return cleared[-1]

        dve_done = part("dve_done")
        act_done = part("act_done")
        var_ready = part("var_ready")
        rstd_ready = part("rstd_ready")
        pad_ready = part("pad_ready")
        ada_mm, ada_copied, ada_turned = part("ada_mm"), part("ada_copied"), part("ada_turned")
        vec_turned, vec_ready = part("vec_turned"), part("vec_ready")
        gate_spread, gate_turned, gate_ready = part("gate_spread"), part("gate_turned"), part("gate_ready")
        xn_ready, h_turned, h_ready = part("xn_ready"), part("h_turned"), part("h_ready")
        proj_done, proj_read_v, proj_read_s = part("proj_done"), part("proj_read_v"), part("proj_read_s")
        nat_ready, qk_turned, qk_copied = part("nat_ready"), part("qk_turned"), part("qk_copied")
        kc_ready = part("kc_ready")
        scored, biased, probs_ready = part("scored"), part("biased"), part("probs_ready")
        p_turned, pt_by_s, pt_by_v, pv_done = part("p_turned"), part("pt_by_s"), part("pt_by_v"), part("pv_done")
        sink_arg, sink_exp, heads_read, merged = part("sink_arg"), part("sink_exp"), part("heads_read"), part("merged")
        side_full, side_free = part("side_full"), part("side_free")
        x_new, xn_new = part("x_new"), part("xn_new")
        logit_max, aff_exp, aff_ready = part("logit_max"), part("aff_exp"), part("aff_ready")
        route_turned, route_ready = part("route_turned"), part("route_ready")
        idx_first, idx_ready = part("idx_first"), part("idx_ready")
        xe_scaled, added = part("xe_scaled"), part("added")
        xe_turned, xe_ready = part("xe_turned"), part("xe_ready")
        gu_done, silu_done, hid_ready = part("gu_done"), part("silu_done"), part("hid_ready")
        hid_turned, hid_copied = part("hid_turned"), part("hid_copied")
        y_done, y_scaled = part("y_done"), part("y_scaled")
        nums = [s.num for s in cleared]
        assert nums == list(range(nums[0], nums[0] + len(nums)))

        def settle(eng):
            eng.sem_inc(passed, 1)

        def wait_e(eng, sem, e, per, n):
            g, j = e
            assert per * j + n + AHEAD > 0
            eng.wait_ge(sem, g * (GROUP * per) + (per * j + n + AHEAD))
            settle(eng)

        def barrier(eng, n):
            eng.drain().then_inc(arrived, 1)
            eng.wait_ge(released, n)
            settle(eng)

        class Chain:
            def __init__(self, eng, done):
                self.eng, self.done, self.n = eng, done, 0

            def add(self, ins):
                self.n += 1
                ins.then_inc(self.done, 1)
                self.eng.wait_ge(self.done, self.n)

        def bc(ap, dims):
            return ap.unsqueeze(2).to_broadcast([ap.shape[0], ap.shape[1], dims])

        block = ctx.enter_context(nc.Block())

        @block.sync
        def _(sp):
            in_v, out_v, ada_v = (w.rearrange("l (k p) f -> l p k f", p=P) for w in (w_in, w_out, w_ada))
            gate_v, up_v, down_v = (w.rearrange("l e (k p) f -> (l e) p k f", p=P) for w in (w_gate, w_up, w_down))

            def load(j, turn, src, at, n):
                sp.wait_ge(slot_free[j], turn * 2 + 1)
                settle(sp)
                sp.dma_start(ring[j][:, :, :], src[bass.ds(at, 1), :, :, 512 * n:512 * n + 512].rearrange("o p k f -> (o p) k f"))\
                    .then_inc(slot_loaded[j], 16)

            with sp.Fori(0, LAYERS) as layer:
                for n in range(ADA // 512):
                    load(n % RING, layer * TURNS + n // RING, ada_v, layer, n)
                turn = layer * TURNS + 2
                for n in range(MIX_CHUNKS):
                    load(n, turn, in_v, layer, n)
                for n in range(2):
                    load(4 + n, turn, out_v, layer, n)
                with sp.Fori(0, EXPERTS) as e:
                    turn = layer * TURNS + e + 3
                    for j, (w, n) in enumerate([(gate_v, 0), (up_v, 0), (gate_v, 1), (up_v, 1), (down_v, 0), (down_v, 1)]):
                        load(j, turn, w, layer * EXPERTS + e, n)

        @block.gpsimd
        def _(pool):
            clear = range(nums[0], nums[-1] + 1)

            def meet(n):
                pool.drain()
                pool.wait_ge(arrived, n * 3)
                settle(pool)
                pool.sem_clear(clear)
                pool.sem_inc(released, 1)

            pool.dma_start(nat[0:2, 0:D], c[:, :]).then_inc(consts_in, 16)
            pool.dma_start(con[:, :], consts[:, :]).then_inc(consts_in, 16)
            pool.memset(neg_half[:, :], -0.5).then_inc(started, 1)
            pool.wait_ge(started, 1)
            pool.memset(aff[:, :, :, :], 0.0).then_inc(started, 1)
            pool.wait_ge(started, 2)
            pool.wait_ge(slot_loaded[1], 16)
            pool.dma_start(x_d[:, :], x[:, :]).then_inc(x_out, 16)
            pool.wait_ge(x_out, 16)
            pool.sem_inc(x_there, 1)

            def powers(at, count, n):
                pool.wait_ge(var_ready, n)
                pool.tensor_tensor(stat[:, 8 + at:8 + at + count], stat[:, at:at + count], neg_half[:, 0:count], ALU.pow)\
                    .then_inc(rstd_ready, 1)

            def prepare(layer):
                pad = xn[0:4 * ROW_OFF, 0:128]
                pool.memset(pad, 0.0).then_inc(pad_ready, 1)
                pool.wait_ge(pad_ready, 1)
                pool.dma_start(xn[0:4 * ROW_OFF, 48:48 + COL_OFF],
                               rpb[bass.ds(layer, 1), :, :, :].rearrange("l h r c -> (l h r) c")).then_inc(skew_in, 16)
                pool.dma_start(router[:, :, :],
                               w_router[bass.ds(layer, 1), :, :].rearrange("l (k p) e -> (l p) k e", p=P)).then_inc(layer_in, 16)
                pool.dma_start(sinks[:, :], sink[bass.ds(layer, 1), :].to_broadcast([P, 8])).then_inc(layer_in, 16)
                for h in range(6):
                    g = q_gain if h < 4 else k_gain
                    pool.dma_start(gain_b[:, h, :], g[bass.ds(layer, 1), :].to_broadcast([P, HD])).then_inc(layer_in, 16)
                pool.wait_ge(skew_in, layer * 16 + 16)
                settle(pool)
                pool.dma_start(skew_d[:, :, :], pad.unsqueeze(1).to_broadcast([4 * ROW_OFF, GRID, 128])).then_inc(skew_out, 16)
                pool.wait_ge(skew_out, layer * 16 + 16)
                settle(pool)
                for h in range(4):
                    for r in range(2):
                        src = bass.AP(skew_d.tensor, (h * ROW_OFF + 1 - r) * GRID * 128 + 63,
                                      [[127, GRID], [GRID * 128, 14], [1, GRID]])
                        pool.dma_start(bias_c[r * GRID:(r + 1) * GRID, h, :, :], src).then_inc(bias_in, 16)

            def attend(layer, s):
                it = layer * SEQS + s
                rows = s * SEQ
                n = 0
                for i in range(TILES + 2):
                    if i < TILES:
                        n += 1
                        powers(0, 1, n)
                    if i >= 2:
                        n += 1
                        powers(0, 6, n)
                for kind, i, k in schedule():
                    if kind == "heads_a":
                        n += 1
                        powers(0, 1, n)
                    if kind == "heads_b":
                        n += 1
                        powers(1, 2, n)
                    if kind == "norm":
                        n += 1
                        pool.wait_ge(x_new, i + 1)
                        pool.dma_start(x_d[bass.ds(rows + i * P, P), :], X[i][:, :]).then_inc(x_out, 16)
                        powers(3, 1, n)
                    if kind == "normed_0":
                        pool.wait_ge(xn_new, i + 1)
                        pool.dma_start(xn_d[bass.ds(rows + i * P, P), :], xn[:, :]).then_inc(xn_out, 16)
                        pool.wait_ge(x_out, it * 64 + 16 * i + 32)
                        settle(pool)
                pool.wait_ge(xn_out, it * 64 + 64)
                settle(pool)

            def gather(j):
                pool.indirect_dma_start(out=X[j][:, :], out_offset=None, in_=xn_d[:, :],
                                        in_offset=bass.IndirectOffsetOnAxis(ap=idx_in[j][:, 0:1], axis=0))\
                    .then_inc(gathered[j], 16)

            def experts(layer, g):
                for j in range(GROUP):
                    e = (g, j)
                    wait_e(pool, xe_turned, e, 2, 2)
                    wait_e(pool, idx_ready, e, 1, 1)
                    gather(j)
                    wait_e(pool, y_scaled, e, 2, 2)
                    pool.indirect_dma_start(out=x_d[:, :],
                                            out_offset=bass.IndirectOffsetOnAxis(ap=idx_out[j][:, 0:1], axis=0),
                                            in_=xn[:, :] if j % 2 else nat[:, 0:D], in_offset=None,
                                            compute_op=ALU.add).then_inc(scattered, 16)
                    pool.wait_ge(scattered, (layer * GROUPS + g) * 64 + (16 * j + 16))
                    pool.sem_inc(added, 1)

            with pool.Fori(0, LAYERS) as layer:
                prepare(layer)
                meet(layer * EPOCHS + 1)
                with pool.Fori(0, SEQS) as s:
                    attend(layer, s)
                    meet(layer * EPOCHS + s + 2)
                meet(layer * EPOCHS + 4)
                pool.sem_inc(added, AHEAD)
                pool.wait_ge(idx_first, 1)
                for j in range(GROUP):
                    gather(j)
                with pool.Fori(0, GROUPS) as g:
                    experts(layer, g)
                for j in range(GROUP):
                    pool.wait_ge(gathered[j], layer * 80 + 80)
                    settle(pool)
                meet(layer * EPOCHS + 5)
                pool.sem_inc(x_there, 1)
            pool.dma_start(gate1[:, :], g_final.rearrange("(a n) -> a n", a=1).to_broadcast([P, D])).then_inc(final_in, 16)
            for t in range(SEQS * TILES):
                powers(0, 1, t + 1)
                pool.wait_ge(xn_new, t + 1)
                pool.dma_start(y[t * P:(t + 1) * P, :], X[t % TILES][:, :]).then_inc(y_out, 16)
                pool.wait_ge(y_out, 16 * (t + 1))

        @block.scalar
        def _(act):
            act.wait_ge(started, 2)
            act.wait_ge(consts_in, 32)
            act.activation(nat[0:2, 0:D], nat[0:2, 0:D], ACT.Silu).then_inc(act_done, 1)
            act.wait_ge(c_turned, 1)
            act.activation(silu_c[:, :, :], bank[0][:, 0:KT * SEQS].rearrange("p (k s) -> p k s", s=SEQS),
                           ACT.Copy).then_inc(xn_ready, 1)

            def ada(layer):
                rows = hT[1][:, 0, :]
                for src, at, n in ((b_ada, R_BIAS, 48), (g_mix, R_GMIX, 8), (g_ffn, R_GFFN, 8), (g_grp, R_GGRP, 8)):
                    act.dma_start(rows[at:at + n, :], src[bass.ds(layer, 1), :].rearrange("o (k p) -> (o k) p", p=P))\
                        .then_inc(rows_in, 16)
                act.wait_ge(x_there, layer + 1)
                settle(act)
                for i in range(TILES):
                    act.dma_start(X[i][:, :], x_d[i * P:(i + 1) * P, :]).then_inc(x_in[i], 16)

            def spread_gate(dst, bank0):
                act.wait_ge(gate_turned, 1)
                act.activation(dst[:, 0:512], bank[bank0][:, :], ACT.Copy)
                act.activation(dst[:, 512:1024], bank[bank0 + 1][:, :], ACT.Copy).then_inc(gate_ready, 1)

            def attend(layer, s):
                it = layer * SEQS + s

                def normed(i):
                    act.wait_ge(vec_ready, 1)
                    if i >= 2:
                        act.wait_ge(proj_done, 4 * (i - 1))
                    for k in range(KT):
                        if k % 4 == 0:
                            act.wait_ge(h_turned, 2 * i + k // 4 + 1)
                        ins = act.activation(hT[i % 2][:, k, :], bank[k // 4][:, (k % 4) * P:(k % 4 + 1) * P],
                                             ACT.Identity, scale=vec[:, M_SC1 + k:M_SC1 + k + 1],
                                             bias=vec[:, M_SH1 + k:M_SH1 + k + 1])
                        if k % 4 == 3:
                            ins.then_inc(h_ready, 1)

                def copies(i):
                    act.wait_ge(proj_done, 4 * i + 3)
                    if i:
                        act.wait_ge(nat_ready, i)
                    act.activation(pbuf[:, 0, 256:384], bank[4][:, 0:128], ACT.Copy)
                    act.activation(V[:, i, 128:256], bank[4][:, 128:256], ACT.Copy)
                    if i:
                        act.wait_ge(qk_turned, 3 * i)
                    act.activation(nat[:, 768:1024], bank[4][:, 256:512], ACT.Copy).then_inc(proj_read_s, 1)
                    act.wait_ge(proj_done, 4 * i + 4)
                    act.activation(nat[:, 1280:1536], bank[5][:, 0:256], ACT.Copy).then_inc(kc_ready, 1)
                    act.activation(V[:, i, 256:512], bank[5][:, 256:512], ACT.Copy).then_inc(proj_read_s, 1)

                def turned(i):
                    for n in range(3):
                        act.wait_ge(qk_turned, 3 * i + n + 1)
                        dst = qT[:, 4 * n:4 * n + 4, i * P:(i + 1) * P] if n < 2 else kT[:, :, i * P:(i + 1) * P]
                        act.activation(dst, bank[6 + n % 2][:, :].rearrange("p (a b) -> p a b", a=4), ACT.Copy,
                                       scale=-(HD ** -0.5) if n < 2 else 1.0).then_inc(qk_copied, 1)

                normed(0)
                for i in range(TILES):
                    if i + 1 < TILES:
                        normed(i + 1)
                    if i == 0:
                        spread_gate(gate1, 6)
                    if i:
                        turned(i - 1)
                    copies(i)
                turned(TILES - 1)

                side = 0
                for kind, i, k in schedule():
                    if kind == "slot":
                        if k < UNITS:
                            u = k % 16
                            grp, *_, st = unit(u)
                            n = keys(i, u)[1] * P
                            act.wait_ge(biased, k + 1)
                            src = bank[k % 3][:, 0:n] if grp == "B" else pbuf[:, k % 3, 0:n]
                            if k >= 3:
                                act.wait_ge(p_turned, k - 2)
                            act.activation(pbuf[:, k % 3, 0:n], src, ACT.Exp, scale=-1.0, bias=smin[:, i % 2, st:st + 1],
                                           accum_out=ssum[:, i % 2, st:st + 1]).then_inc(probs_ready, 1)
                        m = k - T_LAG
                        if 0 <= m < UNITS and m % 2 == 0:
                            n = keys(m // 16, m % 16)[1] * P
                            act.wait_ge(p_turned, m + 1)
                            if m >= 2:
                                act.wait_ge(pv_done, m - 1)
                            act.activation(pbuf[:, 3, 0:n], bank[3][:, 0:n], ACT.Copy).then_inc(pt_by_s, 1)
                    if kind == "sink":
                        act.wait_ge(sink_arg, i + 1)
                        act.activation(stat[:, 16:24], stat[:, 16:24], ACT.Exp).then_inc(sink_exp, 1)
                    if kind in ("normed_0", "normed_1"):
                        half = int(kind[-1])
                        act.wait_ge(side_full, 7 * i + 5 + half)
                        for k4 in range(4):
                            kk = 4 * half + k4
                            ins = act.activation(hT[1][:, kk, :], bank[7][:, k4 * P:(k4 + 1) * P], ACT.Identity,
                                                 scale=vec[:, M_SC2 + kk:M_SC2 + kk + 1],
                                                 bias=vec[:, M_SH2 + kk:M_SH2 + kk + 1])
                        ins.then_inc(side_free, 1)
                    if kind == "router_1":
                        act.wait_ge(x_out, it * 64 + (16 * i + 32))
                        settle(act)
                        act.dma_start(X[i][:, :], x_d[bass.ds((s * -SEQ) + (SEQ + i * P), P), :]).then_inc(x_in[i], 16)

            def experts(g):
                def hidden_copy(e, half):
                    wait_e(act, hid_turned, e, 2, half + 1)
                    if half == 0:
                        wait_e(act, y_done, e, 2, 0)
                    act.activation(hidT[:, 4 * half:4 * half + 4, :],
                                   bank[4 + half][:, :].rearrange("p (a b) -> p a b", a=4), ACT.Copy).then_inc(hid_copied, 1)

                for j in range(GROUP):
                    e = (g, j)
                    for half in range(2):
                        wait_e(act, gu_done, e, 4, 2 * half + 1)
                        act.sem_inc(slot_free[2 * half], 2)
                        wait_e(act, hid_ready, e, 2, half - 1)
                        act.activation(pbuf[:, half, :], bank[half][:, :], ACT.Silu).then_inc(silu_done, 1)
                    hidden_copy(e, 0)
                    hidden_copy(e, 1)

            with act.Fori(0, LAYERS) as layer:
                ada(layer)
                barrier(act, layer * EPOCHS + 1)
                with act.Fori(0, SEQS) as s:
                    attend(layer, s)
                    barrier(act, layer * EPOCHS + s + 2)
                act.wait_ge(logit_max, 1)
                act.activation(probs_r, probs_r, ACT.Exp).then_inc(aff_exp, 1)
                spread_gate(gate2, 2)
                for i in range(TILES):
                    act.wait_ge(x_in[i], layer * 48 + 48)
                    settle(act)
                barrier(act, layer * EPOCHS + 4)
                act.sem_inc(silu_done, AHEAD)
                act.sem_inc(hid_copied, AHEAD)
                with act.Fori(0, GROUPS) as g:
                    experts(g)
                barrier(act, layer * EPOCHS + 5)
            for t in range(SEQS * TILES):
                if t >= TILES:
                    act.wait_ge(y_out, 16 * (t - TILES + 1))
                act.dma_start(X[t % TILES][:, :], x_d[t * P:(t + 1) * P, :]).then_inc(x_in[t % TILES], 16)

        @block.vector
        def _(dve):
            for j in range(2, RING):
                dve.wait_ge(slot_loaded[j - 2], 16)
                dve.sem_inc(slot_free[j], 1)

            def ada(layer):
                chain = Chain(dve, dve_done)
                dve.wait_ge(layer_in, layer * 128 + 128)
                settle(dve)
                chain.add(dve.tensor_scalar(nsink[:, :], sinks[:, :], -1.0, None, ALU.mult))
                dve.wait_ge(vec_turned, 1)
                chain.add(dve.tensor_copy(rows_t[:, :], bank[0][:, 0:R_END]))
                for n in range(12):
                    dve.wait_ge(ada_mm, n + 1)
                    if n >= 2:
                        dve.wait_ge(ada_turned, n - 1)
                    dve.tensor_copy(pbuf[0:2, n % 2, :], bank[2 + n % 2][0:2, :]).then_inc(ada_copied, 1)
                dve.wait_ge(bias_in, layer * 128 + 128)
                settle(dve)
                chain.add(dve.scalar_tensor_tensor(
                    out=bias_c[:, :, :, :].rearrange("p h m c -> p (h m) c"),
                    in0=bias_c[:, :, :, :].rearrange("p h m c -> p (h m) c"), scalar=-1.0,
                    in1=mask_c.unsqueeze(1).to_broadcast([P, 56, GRID]), op0=ALU.mult, op1=ALU.add))
                dve.wait_ge(ada_turned, 12)
                chain.add(dve.tensor_tensor(mods[:, :, :], bank[1][:, 0:M_END * SEQS].rearrange("p (m s) -> p m s", s=SEQS),
                                            bc(rows_t[:, R_BIAS:R_BIAS + M_END], SEQS), ALU.add))
                for sc, g in ((M_SC1, R_GMIX), (M_SC2, R_GFFN)):
                    dve.scalar_tensor_tensor(out=mods[:, sc:sc + 8, :], in0=mods[:, sc:sc + 8, :], scalar=1.0,
                                             in1=bc(rows_t[:, g:g + 8], SEQS), op0=ALU.add, op1=ALU.mult)

            def attend(layer, s):
                it = layer * SEQS + s
                chain = Chain(dve, dve_done)
                rn = [0]

                def rstd(count):
                    rn[0] += 1
                    dve.wait_ge(rstd_ready, rn[0])

                dve.tensor_copy(vec[:, :].unsqueeze(2), mods[:, :, bass.ds(s, 1)]).then_inc(vec_ready, 1)

                def norm(i):
                    dve.wait_ge(x_in[i], layer * 48 + s * 16 + 16)
                    if i:
                        dve.wait_ge(h_turned, 2 * i)
                    settle(dve)
                    dve.tensor_tensor_reduce(xn[:, :], X[i][:, :], X[i][:, :], 1.0 / D, EPS, ALU.mult, ALU.add,
                                             stat[:, 0:1]).then_inc(var_ready, 1)
                    rstd(1)
                    dve.tensor_scalar(xn[:, :], X[i][:, :], stat[:, 8:9], None, ALU.mult).then_inc(xn_ready, 1)

                def rotate(dst, src, cs, heads, half, t2):
                    a, b = src.shape[1], src.shape[2]
                    nb = HD // (2 * half)
                    cos = cs[:, 0:HD].unsqueeze(1).to_broadcast([P, b, HD])
                    for q in range(a):
                        chain.add(dve.tensor_tensor(dst[:, q], src[:, q], cos, ALU.mult))
                        for blk in range(nb):
                            o = blk * 2 * half
                            for lo, hi in ((o, o + half), (o + half, o)):
                                sin = cs[:, HD + lo:HD + lo + half].unsqueeze(1).to_broadcast([P, b, half])
                                ins = dve.tensor_tensor(t2[:, q, :, lo:lo + half], src[:, q, :, hi:hi + half], sin, ALU.mult)
                        chain.add(ins)
                        ins = dve.tensor_tensor(dst[:, q], dst[:, q], t2[:, q], ALU.add)
                    return ins

                def rope(i):
                    r0 = C_ROPE + 256 * i
                    ca, cb = con[:, r0:r0 + 128], con[:, r0 + 128:r0 + 256]
                    flat = pbuf[:, :, :].rearrange("p a b -> p (a b)")
                    t2 = flat[:, 512:1024].rearrange("p (a b d) -> p a b d", a=2, d=HD)
                    dve.wait_ge(proj_done, 4 * i + 1)
                    if i:
                        dve.wait_ge(qk_turned, 3 * i)
                    else:
                        dve.wait_ge(gate_turned, 1)
                    chain.add(rotate(nat[:, 0:512].rearrange("p (j g d) -> p g j d", j=4, g=2),
                                     bank[2][:, :].rearrange("p (g j d) -> p g j d", g=2, j=4), ca, 8, 32, t2))
                    dve.sem_inc(proj_read_v, 1)
                    dve.wait_ge(proj_done, 4 * i + 2)
                    chain.add(rotate(nat[:, 1024:1152].rearrange("p (a b d) -> p a b d", a=1, d=HD),
                                     bank[3][:, 0:128].rearrange("p (a b d) -> p a b d", a=1, d=HD), ca, 2, 32,
                                     flat[:, 512:640].rearrange("p (a b d) -> p a b d", a=1, d=HD)))
                    xb = flat[:, 0:384]
                    dve.tensor_copy(V[:, i, 0:128], bank[3][:, 128:256])
                    dve.tensor_copy(xb[:, 0:256], bank[3][:, 256:512]).then_inc(proj_read_v, 1)
                    dve.wait_ge(proj_read_v, 2 * i + 2)
                    dve.wait_ge(proj_read_s, 2 * i + 1)
                    sq = flat[:, 512:896]
                    xb3 = xb.rearrange("p (h d) -> p h d", d=HD)
                    chain.add(dve.tensor_tensor(sq, xb, xb, ALU.mult))
                    chain.add(dve.tensor_reduce(stat[:, 24:30], sq.rearrange("p (h d) -> p h d", d=HD), AX.X, ALU.add))
                    dve.tensor_scalar(stat[:, 0:6], stat[:, 24:30], 1.0 / HD, EPS, ALU.mult, ALU.add).then_inc(var_ready, 1)
                    rstd(6)
                    chain.add(dve.tensor_tensor(xb3, xb3, bc(stat[:, 8:14], HD), ALU.mult))
                    chain.add(dve.tensor_tensor(xb3, xb3, gain_b[:, :, :], ALU.mult))
                    chain.add(rotate(nat[:, 512:768].rearrange("p (j g d) -> p g j d", j=2, g=2),
                                     xb[:, 0:256].rearrange("p (g j d) -> p g j d", g=2, j=2), cb, 4, 16,
                                     flat[:, 512:768].rearrange("p (a b d) -> p a b d", a=2, d=HD)))
                    rotate(nat[:, 1152:1280].rearrange("p (a b d) -> p a b d", a=1, d=HD),
                           xb[:, 256:384].rearrange("p (a b d) -> p a b d", a=1, d=HD), cb, 2, 16,
                           flat[:, 512:640].rearrange("p (a b d) -> p a b d", a=1, d=HD)).then_inc(nat_ready, 1)

                norm(0)
                dve.wait_ge(vec_ready, 1)
                dve.tensor_copy(nat[:, 0:D].rearrange("p (k m) -> p k m", m=P), bc(vec[:, M_GT1:M_GT1 + 8], P))\
                    .then_inc(gate_spread, 1)
                norm(1)
                for i in range(TILES):
                    if i + 2 < TILES:
                        norm(i + 2)
                    rope(i)

                def ttr_min(out, in0, in1, first, acc):
                    return dve.tensor_tensor_reduce(out, in0, in1, 1.0, first, ALU.add, ALU.min, acc)

                for kind, i, k in schedule():
                    if kind == "slot":
                        if k < UNITS:
                            u = k % 16
                            grp, *_, st = unit(u)
                            lo, nb = keys(i, u)
                            dve.wait_ge(scored, k + 1)
                            if k >= 3:
                                dve.wait_ge(p_turned, k - 2)
                            src, dst, acc = bank[k % 3][:, 0:nb * P], pbuf[:, k % 3, 0:nb * P], smin[:, i % 2, st:st + 1]
                            if grp == "A":
                                off = (lo - (i - 1)) * P
                                ins = ttr_min(dst, src, mask_a[:, off:off + nb * P], nsink[:, st:st + 1], acc)
                            elif grp == "B":
                                ins = dve.tensor_reduce(acc, src, AX.X, ALU.min)
                            else:
                                m = 7 - 2 * i - 1
                                ins = ttr_min(dst, src, bias_c[:, st - 12, m:m + NA_ROWS, :].rearrange("p m c -> p (m c)"),
                                              3e38, acc)
                            ins.then_inc(biased, 1)
                        m = k - T_LAG
                        if 0 <= m < UNITS and m % 2 == 1:
                            n = keys(m // 16, m % 16)[1] * P
                            dve.wait_ge(p_turned, m + 1)
                            if m >= 2:
                                dve.wait_ge(pv_done, m - 1)
                            dve.tensor_copy(pbuf[:, 4, 0:n], bank[4][:, 0:n]).then_inc(pt_by_v, 1)
                    if kind == "sink":
                        dve.wait_ge(biased, 16 * i + 8)
                        dve.tensor_tensor(stat[:, 16:24], smin[:, i % 2, 0:8], sinks[:, :], ALU.add).then_inc(sink_arg, 1)
                    if kind in ("heads_a", "heads_b"):
                        a = kind == "heads_a"
                        half = 0 if a else 1
                        dve.wait_ge(probs_ready, 16 * i + 8 * half + 8)
                        if a:
                            dve.wait_ge(sink_exp, i + 1)
                            chain.add(dve.tensor_tensor(ssum[:, i % 2, 0:8], ssum[:, i % 2, 0:8], stat[:, 16:24], ALU.add))
                        chain.add(dve.reciprocal(rinv[:, 8 * half:8 * half + 8], ssum[:, i % 2, 8 * half:8 * half + 8]))
                        dve.wait_ge(pv_done, 16 * i + 8 * half + 8)
                        if i and a:
                            dve.wait_ge(side_full, 7 * (i - 1) + 2)
                        cols = og[:, 512 * half:512 * half + 512]
                        dve.tensor_tensor(cols.rearrange("p (h d) -> p h d", d=HD),
                                          bank[5 + half][:, :].rearrange("p (h d) -> p h d", d=HD),
                                          bc(rinv[:, 8 * half:8 * half + 8], HD), ALU.mult).then_inc(heads_read, 1)
                        dve.wait_ge(heads_read, 2 * i + half + 1)
                        if i and a:
                            dve.wait_ge(side_full, 7 * (i - 1))
                        if i and not a:
                            dve.wait_ge(side_full, 7 * (i - 1) + 4)
                        junk = hT[1 if a else 0][:, :, :].rearrange("p a b -> p (a b)")
                        for n, (o, w) in enumerate(GROUP_COLS):
                            if (o < 512) == a:
                                ins = dve.tensor_tensor_reduce(junk[:, o:o + w], og[:, o:o + w], og[:, o:o + w], 1.0 / w, EPS,
                                                               ALU.mult, ALU.add, stat[:, n:n + 1])
                        ins.then_inc(var_ready, 1)
                        rn[0] += 1
                    if kind in ("scale_a", "scale_b"):
                        dve.wait_ge(rstd_ready, rn[0])
                        for n, (o, w) in enumerate(GROUP_COLS):
                            if (o < 512) == (kind == "scale_a"):
                                ins = dve.tensor_scalar(og[:, o:o + w], og[:, o:o + w], stat[:, 8 + n:9 + n], None, ALU.mult)
                        ins.then_inc(merged, 1)
                    if kind in ("merged_0", "merged_1"):
                        half = int(kind[-1])
                        dve.wait_ge(side_full, 7 * i + 1 + half)
                        dve.tensor_tensor(hT[0][:, 4 * half:4 * half + 4, :], bank[7][:, :].rearrange("p (a b) -> p a b", a=4),
                                          bc(rows_t[:, R_GGRP + 4 * half:R_GGRP + 4 * half + 4], P), ALU.mult)\
                            .then_inc(side_free, 1)
                    if kind in ("out_03", "out_13"):
                        half = int(kind[4])
                        cols = slice(512 * half, 512 * half + 512)
                        dve.wait_ge(side_full, 7 * i + 3 + half)
                        if i == 0:
                            dve.wait_ge(gate_ready, 1)
                        if i and not half:
                            dve.wait_ge(xn_out, it * 64 + 16 * i)
                            settle(dve)
                        dve.tensor_tensor(xn[:, cols], bank[7][:, :], gate1[:, cols], ALU.mult).then_inc(side_free, 1)
                        dve.wait_ge(side_free, 7 * i + 3 + half)
                        chain.add(dve.tensor_tensor(X[i][:, cols], X[i][:, cols], xn[:, cols], ALU.add))
                        if half:
                            dve.sem_inc(x_new, 1)
                    if kind == "norm":
                        dve.tensor_tensor_reduce(xn[:, :], X[i][:, :], X[i][:, :], 1.0 / D, EPS, ALU.mult, ALU.add,
                                                 stat[:, 3:4]).then_inc(var_ready, 1)
                        rn[0] += 1
                    if kind == "normed":
                        dve.wait_ge(rstd_ready, rn[0])
                        dve.tensor_scalar(xn[:, :], X[i][:, :], stat[:, 11:12], None, ALU.mult).then_inc(xn_new, 1)
                    if kind == "router_1":
                        dve.wait_ge(side_full, 7 * i + 7)
                        dve.tensor_copy(aff[:, i, bass.ds(s, 1), 0:EXPERTS].rearrange("p o e -> p (o e)"),
                                        bank[7][:, 0:EXPERTS]).then_inc(side_free, 1)

            def route():
                chain = Chain(dve, dve_done)
                logits = aff[:, :, :, 0:EXPERTS].rearrange("p t s e -> p (t s) e")
                chain.add(dve.tensor_reduce(soft[:, 0, :], logits, AX.X, ALU.max))
                dve.tensor_tensor(probs_r, logits, bc(soft[:, 0, :], EXPERTS), ALU.subtract).then_inc(logit_max, 1)
                dve.wait_ge(aff_exp, 1)
                chain.add(dve.tensor_reduce(soft[:, 0, :], probs_r, AX.X, ALU.add))
                chain.add(dve.reciprocal(soft[:, 1, :], soft[:, 0, :]))
                dve.tensor_tensor(logits, probs_r, bc(soft[:, 1, :], EXPERTS), ALU.mult).then_inc(aff_ready, 1)
                dve.tensor_copy(nat[:, 0:D].rearrange("p (k m) -> p k m", m=64),
                                bc(mods[:, M_GT2:M_GT2 + 8, :].rearrange("p k s -> p (k s)"), 64)).then_inc(gate_spread, 1)
                dve.wait_ge(route_turned, 1)
                scores = hT[0][0:64, 0:4, :].rearrange("p a b -> p (a b)")
                sel = xn[0:64, 0:2 * CAP]
                found = pbuf[0:64, 0, 0:CAP].bitcast(u32)
                chain.add(dve.tensor_copy(scores, bank[0][0:64, :]))
                for r in range(CAP // 8):
                    top = sel[:, CAP + 8 * r:CAP + 8 * r + 8]
                    chain.add(dve.max(top, scores))
                    chain.add(dve.max_index(found[:, 8 * r:8 * r + 8], top, scores))
                    chain.add(dve.match_replace(out=scores, in_to_replace=top, in_values=scores, imm_value=-1.0))
                dve.tensor_copy(sel[:, 0:CAP], found).then_inc(route_ready, 1)
                dve.wait_ge(route_turned, 2)
                b = bank[1]
                dve.tensor_copy(idx_f[0:64, :], b[0:64, 0:16])
                dve.tensor_scalar(idx_f[64:128, :], b[0:64, 32:48], float(SEQ), None, ALU.add)
                dve.tensor_copy(gate_t[0:64, :], b[64:128, 0:16])
                chain.add(dve.tensor_copy(gate_t[64:128, :], b[64:128, 32:48]))
                dve.memset(idx_t[:, EXPERTS:EXPERTS + GROUP], 0)
                chain.add(dve.tensor_copy(idx_t[:, 0:EXPERTS], idx_f[:, :]))

            def modulate(e, j):
                for half in range(2):
                    wait_e(dve, xe_turned, e, 2, half + 1)
                    if half == 0:
                        wait_e(dve, gu_done, e, 4, -4)
                    dst = hT[j % 2][:, 4 * half:4 * half + 4, :].rearrange("p k (s t) -> p (k s) t", s=SEQS)
                    a = mods[:, M_SC2 + 4 * half:M_SC2 + 4 * half + 4, :].rearrange("p k s -> p (k s)")
                    b = mods[:, M_SH2 + 4 * half:M_SH2 + 4 * half + 4, :].rearrange("p k s -> p (k s)")
                    dve.tensor_tensor(dst, bank[5 - half][:, :].rearrange("p (a b) -> p a b", a=8),
                                      bc(a, 64), ALU.mult).then_inc(xe_scaled, 1)
                    wait_e(dve, xe_scaled, e, 2, half + 1)
                    dve.tensor_tensor(dst, dst, bc(b, 64), ALU.add).then_inc(xe_ready, 1)

            def experts(layer, g):
                for j in range(GROUP):
                    e = (g, j)
                    dve.wait_ge(gathered[j], (layer * (GROUPS + 1) + g) * 16 + 16)
                    settle(dve)
                    dve.tensor_copy(idx_in[j][:, 0:1], idx_t[:, bass.ds(g * GROUP + (j + GROUP), 1)])
                    dve.tensor_copy(idx_out[j][:, 0:1], idx_t[:, bass.ds(g * GROUP + j, 1)])
                    dve.tensor_copy(gate_now[:, j:j + 1], gate_t[:, bass.ds(g * GROUP + j, 1)]).then_inc(idx_ready, 1)
                    for half in range(2):
                        wait_e(dve, silu_done, e, 2, half + 1)
                        wait_e(dve, gu_done, e, 4, 2 * half + 2)
                        dve.sem_inc(slot_free[2 * half + 1], 2)
                        wait_e(dve, hid_turned, e, 2, half - 1)
                        dve.tensor_tensor(pbuf[:, 2 + half, :], pbuf[:, half, :], bank[2 + half][:, :], ALU.mult)\
                            .then_inc(hid_ready, 1)
                    modulate((g, j + 1), j + 1)
                    wait_e(dve, idx_ready, e, 1, 1)
                    wait_e(dve, added, e, 1, -1)
                    dst = xn if j % 2 else nat
                    for half in range(2):
                        wait_e(dve, y_done, e, 2, half + 1)
                        dve.sem_inc(slot_free[4 + half], 2)
                        dve.scalar_tensor_tensor(out=dst[:, 512 * half:512 * half + 512], in0=bank[6 + half][:, :],
                                                 scalar=gate_now[:, j:j + 1], in1=gate2[:, 512 * half:512 * half + 512],
                                                 op0=ALU.mult, op1=ALU.mult).then_inc(y_scaled, 1)

            with dve.Fori(0, LAYERS) as layer:
                ada(layer)
                barrier(dve, layer * EPOCHS + 1)
                with dve.Fori(0, SEQS) as s:
                    attend(layer, s)
                    barrier(dve, layer * EPOCHS + s + 2)
                route()
                barrier(dve, layer * EPOCHS + 4)
                for j in range(GROUP):
                    ins = dve.tensor_copy(idx_in[j][:, 0:1], idx_t[:, j:j + 1])
                ins.then_inc(idx_first, 1)
                for done in (idx_ready, xe_scaled, xe_ready, hid_ready, y_scaled):
                    dve.sem_inc(done, AHEAD)
                modulate((0, 0), 0)
                with dve.Fori(0, GROUPS) as g:
                    experts(layer, g)
                barrier(dve, layer * EPOCHS + 5)
            dve.wait_ge(final_in, 16)
            for t in range(SEQS * TILES):
                dve.wait_ge(x_in[t % TILES], 16 * (LAYERS * (SEQS + 1) + t // TILES + 1))
                xt = X[t % TILES]
                dve.tensor_tensor_reduce(xn[:, :], xt[:, :], xt[:, :], 1.0 / D, EPS, ALU.mult, ALU.add,
                                         stat[:, 0:1]).then_inc(var_ready, 1)
                dve.wait_ge(rstd_ready, t + 1)
                dve.scalar_tensor_tensor(out=xt[:, :], in0=xt[:, :], scalar=stat[:, 8:9], in1=gate1[:, :],
                                         op0=ALU.mult, op1=ALU.mult).then_inc(xn_new, 1)

        @block.tensor
        def _(pe):
            for j in range(2):
                pe.sem_inc(slot_free[j], 1)
            pe.wait_ge(started, 2)
            pe.wait_ge(act_done, 1)
            for k in range(KT):
                ins = pe.transpose(bank[0][:, SEQS * k:SEQS * (k + 1)], nat[0:2, k * P:(k + 1) * P], ident[0:2, 0:2])
            ins.then_inc(c_turned, 1)
            pe.wait_ge(xn_ready, 1)

            def use(j, turn):
                pe.wait_ge(slot_loaded[j], turn * 16 + 16)
                settle(pe)

            def ada(layer):
                def turn_ada(n):
                    pe.wait_ge(ada_copied, n + 1)
                    for m in range(4):
                        o = SEQS * (4 * n + m)
                        ins = pe.transpose(bank[1][:, o:o + SEQS], pbuf[0:2, n % 2, m * P:(m + 1) * P], ident[0:2, 0:2])
                    ins.then_inc(ada_turned, 1)

                for n in range(12):
                    use(n % RING, layer * TURNS + n // RING)
                    if n >= 2:
                        pe.wait_ge(ada_copied, n - 1)
                    for k in range(KT):
                        ins = pe.matmul(bank[2 + n % 2][0:2, :], silu_c[:, k, :], ring[n % RING][:, k, :],
                                        start=(k == 0), stop=(k == KT - 1))
                    ins.then_inc(ada_mm, 1)
                    if n:
                        turn_ada(n - 1)
                        pe.sem_inc(slot_free[(n - 1) % RING], 2)
                    else:
                        pe.wait_ge(rows_in, layer * 64 + 64)
                        settle(pe)
                        pe.transpose(bank[0][:, 0:R_END], hT[1][0:R_END, 0, :], ident[0:R_END, 0:R_END]).then_inc(vec_turned, 1)
                turn_ada(11)
                pe.sem_inc(slot_free[RING - 1], 2)

            def spread_gate(bank0):
                pe.wait_ge(gate_spread, 1)
                for k in range(KT):
                    ins = pe.matmul(bank[bank0 + k // 4][:, (k % 4) * P:(k % 4 + 1) * P], nat[:, k * P:(k + 1) * P], ident,
                                    start=True, stop=True)
                ins.then_inc(gate_turned, 1)

            def attend(layer, s):
                it = layer * SEQS + s
                turn = layer * TURNS + 2
                def turn_h(i):
                    pe.wait_ge(xn_ready, i + 1)
                    for k in range(KT):
                        if k % 4 == 0 and i:
                            pe.wait_ge(h_ready, 2 * i - 1 + k // 4)
                        ins = pe.transpose(bank[k // 4][:, (k % 4) * P:(k % 4 + 1) * P], xn[:, k * P:(k + 1) * P], ident)
                        if k % 4 == 3:
                            ins.then_inc(h_turned, 1)

                def turn_qk(i):
                    pe.wait_ge(nat_ready, i + 1)
                    pe.wait_ge(kc_ready, i + 1)
                    if i == 0:
                        pe.wait_ge(gate_ready, 1)
                    for n in range(3):
                        if 3 * i + n >= 2:
                            pe.wait_ge(qk_copied, 3 * i + n - 1)
                        if n == 0 and i:
                            pe.wait_ge(qk_copied, 3 * i)
                        for a in range(4):
                            o = 512 * n + P * a
                            ins = pe.transpose(bank[6 + n % 2][:, a * P:(a + 1) * P], nat[:, o:o + P], ident)
                        ins.then_inc(qk_turned, 1)

                turn_h(0)
                for i in range(TILES):
                    if i + 1 < TILES:
                        turn_h(i + 1)
                    if i == 0:
                        spread_gate(6)
                    pe.wait_ge(h_ready, 2 * i + 2)
                    for ch in range(MIX_CHUNKS):
                        if i == 0:
                            use(ch, turn)
                        else:
                            pe.wait_ge(proj_read_v if ch < 2 else proj_read_s, 2 * (i - 1) + ch % 2 + 1)
                        for k in range(KT):
                            ins = pe.matmul(bank[2 + ch][:, :], hT[i % 2][:, k, :], ring[ch][:, k, :],
                                            start=(k == 0), stop=(k == KT - 1))
                        ins.then_inc(proj_done, 1)
                        if i and ch == 1:
                            turn_qk(i - 1)
                pe.wait_ge(proj_done, 4 * TILES)
                for ch in range(MIX_CHUNKS):
                    pe.sem_inc(slot_free[ch], 1)
                turn_qk(TILES - 1)
                pe.wait_ge(proj_read_v, 2 * TILES)
                pe.wait_ge(proj_read_s, 2 * TILES)
                pe.wait_ge(qk_copied, 3 * TILES)
                use(4, turn)
                use(5, turn)

                side = 0

                def side_turn(i):
                    if side:
                        pe.wait_ge(side_free, side)

                for kind, i, k in schedule():
                    if kind == "slot":
                        if k < UNITS:
                            grp, qp, g, kp, _, _, _ = unit(k % 16)
                            lo, nb = keys(i, k % 16)
                            if k >= 3:
                                pe.wait_ge(probs_ready, k - 2)
                            rows = slice(HD * g, HD * g + HD)
                            pe.matmul(bank[k % 3][:, 0:nb * P], qT[rows, qp, i * P:(i + 1) * P],
                                      kT[rows, kp, lo * P:(lo + nb) * P], start=True, stop=True).then_inc(scored, 1)
                        m = k - T_LAG
                        if 0 <= m < UNITS:
                            nb = keys(m // 16, m % 16)[1]
                            pe.wait_ge(probs_ready, m + 1)
                            if m >= 2:
                                pe.wait_ge(pt_by_v if m % 2 else pt_by_s, m // 2)
                            for b in range(nb):
                                ins = pe.transpose(bank[3 + m % 2][:, b * P:(b + 1) * P], pbuf[:, m % 3, b * P:(b + 1) * P], ident)
                            ins.then_inc(p_turned, 1)
                        m = k - V_LAG
                        if 0 <= m < UNITS:
                            _, _, _, _, vc, oc, _ = unit(m % 16)
                            lo, nb = keys(m // 16, m % 16)
                            pe.wait_ge(pt_by_v if m % 2 else pt_by_s, m // 2 + 1)
                            if m % 8 == 0 and m >= 16:
                                pe.wait_ge(heads_read, m // 8 - 1)
                            for b in range(nb):
                                ins = pe.matmul(bank[5 + oc // 512][:, oc % 512:oc % 512 + HD],
                                                pbuf[:, 3 + m % 2, b * P:(b + 1) * P], V[:, lo + b, vc:vc + HD],
                                                start=(b == 0), stop=(b == nb - 1))
                            ins.then_inc(pv_done, 1)
                    if kind in ("merged_0", "merged_1"):
                        half = int(kind[-1])
                        side_turn(i)
                        pe.wait_ge(merged, 2 * i + 1 + half)
                        for a in range(4):
                            o = 512 * half + P * a
                            ins = pe.transpose(bank[7][:, a * P:(a + 1) * P], og[:, o:o + P], ident)
                        ins.then_inc(side_full, 1)
                        side += 1
                    if kind.startswith("out_"):
                        half, quarter = int(kind[4]), int(kind[5])
                        if quarter == 0:
                            side_turn(i)
                        for kk in range(2 * quarter, 2 * quarter + 2):
                            ins = pe.matmul(bank[7][:, :], hT[0][:, kk, :], ring[4 + half][:, kk, :],
                                            start=(kk == 0), stop=(kk == KT - 1))
                        if quarter == 3:
                            ins.then_inc(side_full, 1)
                            side += 1
                    if kind in ("normed_0", "normed_1"):
                        half = int(kind[-1])
                        side_turn(i)
                        pe.wait_ge(xn_new, i + 1)
                        for a in range(4):
                            o = 512 * half + P * a
                            ins = pe.transpose(bank[7][:, a * P:(a + 1) * P], xn[:, o:o + P], ident)
                        ins.then_inc(side_full, 1)
                        side += 1
                    if kind in ("router_0", "router_1"):
                        half = int(kind[-1])
                        if not half:
                            side_turn(i)
                        for kk in range(4 * half, 4 * half + 4):
                            ins = pe.matmul(bank[7][:, 0:EXPERTS], hT[1][:, kk, :], router[:, kk, :],
                                            start=(kk == 0), stop=(kk == KT - 1))
                        if half:
                            ins.then_inc(side_full, 1)
                            side += 1
                pe.wait_ge(side_full, side)
                pe.sem_inc(slot_free[4], 1)
                pe.sem_inc(slot_free[5], 1)

            def route():
                pe.wait_ge(aff_ready, 1)
                for t in range(TILES):
                    ins = pe.transpose(bank[0][0:64, t * P:(t + 1) * P], aff[:, t, :, :].rearrange("p s e -> p (s e)"), ident)
                ins.then_inc(route_turned, 1)
                spread_gate(2)
                pe.wait_ge(route_ready, 1)
                pe.transpose(bank[1][:, 0:64], xn[0:64, 0:2 * CAP], ident[0:64, 0:64]).then_inc(route_turned, 1)

            def turn_xe(layer, e, j):
                pe.wait_ge(gathered[j % GROUP], (layer * (GROUPS + 1) + e[0]) * 16 + (j // GROUP * 16 + 16))
                settle(pe)
                for half in range(2):
                    wait_e(pe, hid_copied, e, 2, -2 if half == 0 else -1)
                    for a in range(4):
                        o = 512 * half + P * a
                        ins = pe.transpose(bank[5 - half][:, a * P:(a + 1) * P], X[j % GROUP][:, o:o + P], ident)
                    ins.then_inc(xe_turned, 1)

            def experts(layer, g):
                def turn_hid(e, half):
                    wait_e(pe, hid_ready, e, 2, half + 1)
                    wait_e(pe, xe_ready, e, 2, 2 + half)
                    for a in range(4):
                        ins = pe.transpose(bank[4 + half][:, a * P:(a + 1) * P], pbuf[:, 2 + half, a * P:(a + 1) * P], ident)
                    ins.then_inc(hid_turned, 1)

                for j in range(GROUP):
                    e = (g, j)
                    turn = layer * TURNS + g * GROUP + (j + 3)
                    wait_e(pe, xe_ready, e, 2, 2)
                    for n in range(4):
                        half = n // 2
                        use(n, turn)
                        if n % 2 == 0:
                            wait_e(pe, hid_ready, e, 2, half - 1)
                        for k in range(KT):
                            ins = pe.matmul(bank[2 * (n % 2) + half][:, :], hT[j % 2][:, k, :], ring[n][:, k, :],
                                            start=(k == 0), stop=(k == KT - 1))
                        ins.then_inc(gu_done, 1)
                    turn_hid(e, 0)
                    turn_xe(layer, (g, j + 1), j + 1)
                    use(4, turn)
                    use(5, turn)
                    wait_e(pe, y_scaled, e, 2, 0)
                    wait_e(pe, hid_copied, e, 2, 1)
                    for part_k in range(2):
                        if part_k:
                            turn_hid(e, 1)
                            wait_e(pe, hid_copied, e, 2, 2)
                        for half in range(2):
                            for k in range(4 * part_k, 4 * part_k + 4):
                                ins = pe.matmul(bank[6 + half][:, :], hidT[:, k, :], ring[4 + half][:, k, :],
                                                start=(k == 0), stop=(k == KT - 1))
                            if part_k:
                                ins.then_inc(y_done, 1)

            with pe.Fori(0, LAYERS) as layer:
                ada(layer)
                barrier(pe, layer * EPOCHS + 1)
                with pe.Fori(0, SEQS) as s:
                    attend(layer, s)
                    barrier(pe, layer * EPOCHS + s + 2)
                route()
                barrier(pe, layer * EPOCHS + 4)
                for done in (xe_turned, gu_done, hid_turned, y_done):
                    pe.sem_inc(done, AHEAD)
                turn_xe(layer, (0, 0), 0)
                with pe.Fori(0, GROUPS) as g:
                    experts(layer, g)
                barrier(pe, layer * EPOCHS + 5)


def constants():
    import numpy as np
    f = np.float32
    out = np.zeros((P, C_END), f)
    out[:, C_ID:C_ID + P] = np.eye(P, dtype=f)
    q, k = np.arange(P)[:, None], np.arange(P)[None, :]
    out[:, C_MASKA:C_MASKA + P] = np.where(k >= q, 0, BIG)
    out[:, C_MASKA + 2 * P:C_MASKA + 3 * P] = np.where(k <= q, 0, BIG)
    col = np.arange(P)[:, None] % GRID
    start = np.clip(col - 8, 0, GRID - 16)
    kc = np.arange(GRID)[None, :]
    out[:, C_MASKC:C_MASKC + GRID] = np.where((kc >= start) & (kc < start + 16), 0, BIG)

    def table(pos, dim):
        inv = f(10000.0) ** (-np.arange(0, dim, 2, dtype=f) / f(dim))
        ang = pos.astype(f)[:, None] * inv[None, :].astype(f)
        return np.concatenate([np.cos(ang)] * 2, 1), np.concatenate([-np.sin(ang), np.sin(ang)], 1)

    t = np.arange(SEQ)
    ca, sa = table(t, HD)
    cr, sr = table(t // GRID, HD // 2)
    cc, sc = table(t % GRID, HD // 2)
    rope = np.concatenate([ca, sa, cr, cc, sr, sc], 1).astype(f)
    for i in range(TILES):
        out[:, C_ROPE + 256 * i:C_ROPE + 256 * (i + 1)] = rope[i * P:(i + 1) * P]
    return out


_NAMES = ["w_ada", "b_ada", "g_mix", "w_in", "sink", "q_gain", "k_gain", "rpb", "g_grp", "w_out", "g_ffn", "w_router",
          "w_gate", "w_up", "w_down", "g_final"]


def kernel(**inputs):
    import numpy as np
    import concourse.bacc as _bacc
    from concourse.bass_utils import run_bass_kernel_spmd as _run

    nc = _bacc.Bacc("TRN2", target_bir_lowering=False, num_devices=1)
    data = {
        "x": np.concatenate([np.asarray(inputs["x_prompt"]).reshape(SEQ, D), np.asarray(inputs["x_sample"]).reshape(SEQ, D)]),
        "c": np.concatenate([np.asarray(inputs["c_prompt"]), np.asarray(inputs["c_sample"])]),
    }
    for name in _NAMES:
        data[name] = np.ascontiguousarray(inputs[name])
    data["consts"] = constants()
    arrays, args = {}, []
    for name, a in data.items():
        arrays[f"in_{name}"] = a
        args.append(nc.dram_tensor(f"in_{name}", a.shape, mybir.dt.from_np(a.dtype), kind="ExternalInput").ap())
    args.append(nc.dram_tensor("out_y", (SEQS * SEQ, D), mybir.dt.float32, kind="ExternalOutput").ap())
    trunk(nc, *args)
    got = _run(nc, [arrays], core_ids=[0]).results[0]["out_y"]
    return got[0:SEQ].reshape(1, SEQ, D), got[SEQ:].reshape(1, SEQ, D)
```

```python
import numpy as np
import concourse.bass as bass
from concourse import mybir
from contextlib import ExitStack

LAYERS, SEQS, SEQ, D = 2, 2, 512, 1024
HD = 64
P = 128
KT = D // P
TILES = SEQ // P
MIX_CHUNKS = 4
ADA = 6 * D
EXPERTS, CAP = 16, 64
GROUP = 4
GROUPS = EXPERTS // GROUP
RING = 6
GRID, NA_ROWS, ROW_OFF, COL_OFF = 64, 8, 15, 31
TURNS = ADA // 512 // RING + SEQS + EXPERTS
EPOCHS = 1 + SEQS + 1 + 1
AHEAD = 8
EPS = 1e-6
GROUP_COLS = ((0, 512), (512, 256), (768, 256))
BIG = 1e30
UNITS = 16 * TILES
T_LAG, V_LAG = 2, 3
SPLIT_FROM = 8

C_ID, C_MASKA, C_MASKC, C_ROPE, C_END = 0, 128, 512, 576, 1600
M_SH1, M_SC1, M_GT1, M_SH2, M_SC2, M_GT2, M_END = 0, 8, 16, 24, 32, 40, 48
R_BIAS, R_GMIX, R_GFFN, R_GGRP, R_END = 0, 48, 56, 64, 72


def unit(u):
    if u < 8:
        j, g = u // 2, u % 2
        h = 4 * g + j
        return "A", j, g, 0, g * HD, h * HD, h
    if u < 12:
        j, g = (u - 8) // 2, u % 2
        h = 2 * g + j
        return "B", 4 + j, g, 1, 128 + g * HD, 512 + h * HD, 8 + h
    j, g = (u - 12) // 2, u % 2
    h = 2 * j + g
    return "C", 6 + j, g, 2 + j, 256 + h * HD, 768 + h * HD, 12 + h


def keys(i, u):
    if u < 8:
        lo, hi = max(i - 1, 0), min(i + 1, TILES - 1)
        return lo, hi - lo + 1
    return 0, TILES


AFTER = [(8, "sink"), (8 + V_LAG, "heads_a"), (9 + V_LAG, "scale_a"), (15 + V_LAG, "heads_b"), (17 + V_LAG, "scale_b"),
         (20, "merged_0"), (21, "split_0"), (22, "merged_1"), (23, "split_1")]
AFTER += [(23 + 4 * half + quarter, f"out_{half}{quarter}") for half in range(2) for quarter in range(4)]
AFTER += [(31, "norm"), (32, "normed"), (33, "normed_0"), (34, "normed_1"), (35, "router_0"), (36, "router_1")]
SLOTS = 16 * (TILES - 1) + AFTER[-1][0] + 1


def chunks(i):
    return (0, 1, 2, 3) if i == 0 else (2, 1, 0, 3)


def projected(i, ch):
    return MIX_CHUNKS * i + chunks(i).index(ch) + 1


def schedule():
    out = []
    for k in range(SLOTS):
        out.append(("slot", k // 16, k))
        if 4 <= k <= 6:
            out.append((("gate_columns", "gate_rows", "gate_copy")[k - 4], 0, k))
        for i in range(TILES):
            out += [(name, i, k) for at, name in AFTER if 16 * i + at == k]
    return out


def trunk(nc, x, c, w_ada, b_ada, g_mix, w_in, sink, q_gain, k_gain, rpb, g_grp, w_out, g_ffn, w_router,
          w_gate, w_up, w_down, g_final, consts, y):
    f32, f32r, u32 = mybir.dt.float32, mybir.dt.float32r, mybir.dt.uint32
    ALU, ACT, AX = mybir.AluOpType, mybir.ActivationFunctionType, mybir.AxisListType
    ctx, place = ExitStack(), {}
    with ctx:
        def sb(name, shape, dt=f32):
            t = ctx.enter_context(nc.sbuf_tensor(name, shape, dt))
            place[name] = nc.sbuf_base - 4 * int(np.prod(shape[1:]))
            return t

        def rounded(name, shape, at):
            return nc.alloc_sbuf_tensor_at(name, shape, mybir.dt.float32r, offset=at)

        def sem(name):
            return ctx.enter_context(nc.semaphore(name))

        x_d = nc.dram_tensor("residual", [SEQS * SEQ, D], f32).ap()
        xn_d = nc.dram_tensor("normed", [SEQS * SEQ, D], f32).ap()
        skew_d = nc.dram_tensor("bias_rows", [4 * ROW_OFF, GRID, 128], f32).ap()

        ring = [sb(f"ring{j}", [P, KT, 512]) for j in range(RING)]
        con = sb("con", [P, C_END])
        ident = con[:, C_ID:C_ID + P]
        mask_a = con[:, C_MASKA:C_MASKA + 3 * P]
        mask_c = con[:, C_MASKC:C_MASKC + GRID]
        silu_c = sb("silu_c", [P, KT, SEQS])
        rows_t = sb("rows_t", [P, R_END])
        mods = sb("mods", [P, M_END, SEQS])
        vec = sb("vec", [P, M_END])
        gate = sb("gate", [P, D])
        merged_hi = sb("merged_hi", [P, KT, P], f32r)
        bias_c = sb("bias_c", [P, 4, 14, GRID])
        router = sb("router_w", [P, KT, EXPERTS])
        gain_b = sb("gain_b", [P, 6, HD])
        nsink = sb("nsink", [P, 8])
        sinks = sb("sinks", [P, 8])
        neg_half = sb("neg_half", [P, 8])
        aff = sb("aff", [P, TILES, SEQS, 32])
        qT = sb("qT", [P, 8, SEQ])
        kT = sb("kT", [P, 4, SEQ])
        V = sb("V", [P, TILES, 512])
        X = [sb(f"X{i}", [P, D]) for i in range(TILES)]
        xn = sb("xn", [P, D])
        hT = [sb(f"hT{i}", [P, KT, P]) for i in range(2)]
        h_lo_half = sb("h_lo_half", [P, 4, P])
        nat = sb("nat", [P, 1536])
        og = nat[:, 0:D]
        pbuf = sb("pbuf", [P, 5, 512])
        stat = sb("stat", [P, 32])
        smin = sb("smin", [P, 2, 16])
        ssum = sb("ssum", [P, 2, 16])
        rinv = sb("rinv", [P, 16])
        soft = sb("soft", [P, 2, TILES * SEQS])
        idx_t = sb("idx_t", [P, EXPERTS + GROUP], u32)
        idx_f = sb("idx_f", [P, EXPERTS])
        gate_t = sb("gate_t", [P, EXPERTS])
        idx_in = [sb(f"idx_in{j}", [P, 1], u32) for j in range(GROUP)]
        idx_out = [sb(f"idx_out{j}", [P, 1], u32) for j in range(GROUP)]
        gate_now = sb("gate_now", [P, GROUP])
        last = [X[t][:, :] if t < TILES else ring[0][:, 2 * (t - TILES):2 * (t - TILES) + 2, :].rearrange("p a b -> p (a b)")
                for t in range(SEQS * TILES)]
        h_hi = [merged_hi, rounded("h_hi1", [P, KT, P], place["gate"])]
        h_lo = [[rounded(f"h_lo{n}", [P, 4, P], at) for n, at in pair]
                for pair in (((0, place["pbuf"] + 4 * 1024), (1, place["h_lo_half"])),
                             ((2, place["pbuf"] + 4 * 1536), (3, place["pbuf"] + 4 * 2048)))]
        ring_r = [rounded(f"ring_r{j}", [P, KT, 512], place[f"ring{j}"]) for j in range(RING)]
        down_hi = [[rounded("down_hi00", [P, 4, 512], place["qT"]), rounded("down_hi01", [P, 4, 512], place["qT"] + 8192)],
                   [rounded("down_hi10", [P, 4, 512], place["V"]), rounded("down_hi11", [P, 4, 512], place["bias_c"])]]
        hid_hi = rounded("hid_hi", [P, KT, P], place["kT"])
        hid_lo = rounded("hid_lo", [P, KT, P], place["kT"] + 4096)
        merged_lo = rounded("merged_lo", [P, KT, P], place["hT0"])
        probs_r = pbuf[:, 4, 0:TILES * SEQS * EXPERTS].rearrange("p (t e) -> p t e", e=EXPERTS)
        bank = [ctx.enter_context(nc.psum_tensor(f"bank{i}", [P, 512], f32)) for i in range(8)]

        slot_loaded = [sem(f"slot_loaded{j}") for j in range(RING)]
        slot_free = [sem(f"slot_free{j}") for j in range(RING)]
        c_turned = sem("c_turned")
        started = sem("started")
        consts_in, passed = sem("consts_in"), sem("passed")
        arrived, released = sem("arrived"), sem("released")
        layer_in = sem("layer_in")
        skew_in, skew_out, bias_in = sem("skew_in"), sem("skew_out"), sem("bias_in")
        rows_in = sem("rows_in")
        final_in = sem("final_in")
        x_in = [sem(f"x_in{i}") for i in range(TILES)]
        x_out, xn_out = sem("x_out"), sem("xn_out")
        x_there = sem("x_there")
        gathered = [sem(f"gathered{j}") for j in range(GROUP)]
        scattered = sem("scattered")
        last_in = [sem(f"last_in{i}") for i in range(TILES)]
        y_out = sem("y_out")

        cleared = []

        def part(name):
            cleared.append(sem(name))
            return cleared[-1]

        dve_done = part("dve_done")
        act_done = part("act_done")
        var_ready = part("var_ready")
        rstd_ready = part("rstd_ready")
        pad_ready = part("pad_ready")
        ada_mm, ada_copied, ada_turned = part("ada_mm"), part("ada_copied"), part("ada_turned")
        vec_turned, vec_ready = part("vec_turned"), part("vec_ready")
        gate_spread, gate_turned, gate_ready = part("gate_spread"), part("gate_turned"), part("gate_ready")
        xn_ready, h_turned, h_ready = part("xn_ready"), part("h_turned"), part("h_ready")
        proj_done, proj_read_v, proj_read_s = part("proj_done"), part("proj_read_v"), part("proj_read_s")
        in_hi, in_lo = part("in_hi"), part("in_lo")
        h_hi_ready, h_lo_ready = part("h_hi_ready"), part("h_lo_ready")
        nat_ready, qk_turned, qk_copied = part("nat_ready"), part("qk_turned"), part("qk_copied")
        kc_ready = part("kc_ready")
        bias_ready = part("bias_ready")
        scored, biased, probs_ready = part("scored"), part("biased"), part("probs_ready")
        p_turned, pt_by_s, pt_by_v, pv_done = part("p_turned"), part("pt_by_s"), part("pt_by_v"), part("pv_done")
        sink_arg, sink_exp, heads_read, merged = part("sink_arg"), part("sink_exp"), part("heads_read"), part("merged")
        side_full, side_free = part("side_full"), part("side_free")
        out_hi, out_lo = part("out_hi"), [part("out_lo0"), part("out_lo1")]
        merged_hi_ready, merged_lo_ready = part("merged_hi_ready"), part("merged_lo_ready")
        x_new, xn_new = part("x_new"), part("xn_new")
        logit_max, aff_exp, aff_ready = part("logit_max"), part("aff_exp"), part("aff_ready")
        route_turned, route_ready = part("route_turned"), part("route_ready")
        idx_first, idx_ready = part("idx_first"), part("idx_ready")
        xe_scaled, added = part("xe_scaled"), part("added")
        xe_turned, xe_ready = part("xe_turned"), part("xe_ready")
        gu_done, silu_done, hid_ready = part("gu_done"), part("silu_done"), part("hid_ready")
        hid_turned, hid_copied, hid_split = part("hid_turned"), part("hid_copied"), part("hid_split")
        down_hi_ready, down_lo_ready = part("down_hi_ready"), part("down_lo_ready")
        y_done, y_scaled = part("y_done"), part("y_scaled")
        nums = [s.num for s in cleared]
        assert nums == list(range(nums[0], nums[0] + len(nums)))

        def settle(eng):
            eng.sem_inc(passed, 1)

        def wait_e(eng, sem, e, per, n):
            g, j = e
            assert per * j + n + AHEAD > 0
            eng.wait_ge(sem, g * (GROUP * per) + (per * j + n + AHEAD))
            settle(eng)

        def split_out(eng, n):
            half, kk = n // KT, n % KT
            eng.wait_ge(out_hi, n + 1)
            eng.tensor_tensor(ring_r[4 + half][:, kk, :], ring[4 + half][:, kk, :], full(ring_r[2 + half][:, kk, :]),
                              ALU.subtract).then_inc(out_lo[half], 1)

        def barrier(eng, n):
            eng.drain().then_inc(arrived, 1)
            eng.wait_ge(released, n)
            settle(eng)

        class Chain:
            def __init__(self, eng, done):
                self.eng, self.done, self.n = eng, done, 0

            def add(self, ins):
                self.n += 1
                ins.then_inc(self.done, 1)
                self.eng.wait_ge(self.done, self.n)

        def full(ap):
            return ap.bitcast(f32)

        def bc(ap, dims):
            return ap.unsqueeze(2).to_broadcast([ap.shape[0], ap.shape[1], dims])

        block = ctx.enter_context(nc.Block())

        @block.sync
        def _(sp):
            in_v, out_v, ada_v = (w.rearrange("l (k p) f -> l p k f", p=P) for w in (w_in, w_out, w_ada))
            gate_v, up_v, down_v = (w.rearrange("l e (k p) f -> (l e) p k f", p=P) for w in (w_gate, w_up, w_down))

            def load(j, turn, src, at, n):
                sp.wait_ge(slot_free[j], turn * 2 + 1)
                settle(sp)
                sp.dma_start(ring[j][:, :, :], src[bass.ds(at, 1), :, :, 512 * n:512 * n + 512].rearrange("o p k f -> (o p) k f"))\
                    .then_inc(slot_loaded[j], 16)

            with sp.Fori(0, LAYERS) as layer:
                for n in range(ADA // 512):
                    load(n % RING, layer * TURNS + n // RING, ada_v, layer, n)
                with sp.Fori(0, SEQS) as s:
                    turn = layer * TURNS + s + 2
                    for n in range(MIX_CHUNKS):
                        load(n, turn, in_v, layer, n)
                    sp.wait_ge(skew_out, layer * 16 + 16)
                    settle(sp)
                    sp.wait_ge(released, layer * EPOCHS + s + 1)
                    settle(sp)
                    for h in range(4):
                        for r in range(2):
                            src = bass.AP(skew_d.tensor, (h * ROW_OFF + 1 - r) * GRID * 128 + 63,
                                          [[127, GRID], [GRID * 128, 14], [1, GRID]])
                            sp.dma_start(bias_c[r * GRID:(r + 1) * GRID, h, :, :], src).then_inc(bias_in, 16)
                    for n in range(2):
                        load(4 + n, turn, out_v, layer, n)
                with sp.Fori(0, EXPERTS) as e:
                    turn = layer * TURNS + e + (2 + SEQS)
                    for j, (w, n) in enumerate([(gate_v, 0), (up_v, 0), (gate_v, 1), (up_v, 1), (down_v, 0), (down_v, 1)]):
                        load(j, turn, w, layer * EXPERTS + e, n)
            sp.wait_ge(released, LAYERS * EPOCHS)
            for t in range(SEQS * TILES):
                sp.wait_ge(xn_new, t + 1)
                sp.dma_start(y[t * P:(t + 1) * P, :], last[t]).then_inc(y_out, 16)
            sp.wait_ge(y_out, 16 * SEQS * TILES)

        @block.gpsimd
        def _(pool):
            clear = range(nums[0], nums[-1] + 1)

            def meet(n, quiet=False):
                if not quiet:
                    pool.drain()
                pool.wait_ge(arrived, n * 3)
                settle(pool)
                pool.sem_clear(clear)
                pool.sem_inc(released, 1)

            pool.dma_start(nat[0:2, 0:D], c[:, :]).then_inc(consts_in, 16)
            pool.dma_start(con[:, :], consts[:, :]).then_inc(consts_in, 16)
            pool.memset(neg_half[:, :], -0.5).then_inc(started, 1)
            pool.wait_ge(started, 1)
            pool.memset(aff[:, :, :, :], 0.0).then_inc(started, 1)
            pool.wait_ge(started, 2)
            pool.wait_ge(slot_loaded[3], 16)
            pool.dma_start(x_d[SEQ:SEQS * SEQ, :], x[SEQ:SEQS * SEQ, :]).then_inc(scattered, 16)

            def powers(at, count, n):
                pool.wait_ge(var_ready, n)
                pool.tensor_tensor(stat[:, 8 + at:8 + at + count], stat[:, at:at + count], neg_half[:, 0:count], ALU.pow)\
                    .then_inc(rstd_ready, 1)

            def prepare(layer):
                pad = xn[0:4 * ROW_OFF, 0:128]
                pool.memset(pad, 0.0).then_inc(pad_ready, 1)
                pool.wait_ge(pad_ready, 1)
                pool.dma_start(xn[0:4 * ROW_OFF, 48:48 + COL_OFF],
                               rpb[bass.ds(layer, 1), :, :, :].rearrange("l h r c -> (l h r) c")).then_inc(skew_in, 16)
                pool.dma_start(router[:, :, :],
                               w_router[bass.ds(layer, 1), :, :].rearrange("l (k p) e -> (l p) k e", p=P)).then_inc(layer_in, 16)
                pool.dma_start(sinks[:, :], sink[bass.ds(layer, 1), :].to_broadcast([P, 8])).then_inc(layer_in, 16)
                for h in range(6):
                    g = q_gain if h < 4 else k_gain
                    pool.dma_start(gain_b[:, h, :], g[bass.ds(layer, 1), :].to_broadcast([P, HD])).then_inc(layer_in, 16)
                pool.wait_ge(skew_in, layer * 16 + 16)
                settle(pool)
                pool.dma_start(skew_d[:, :, :], pad.unsqueeze(1).to_broadcast([4 * ROW_OFF, GRID, 128])).then_inc(skew_out, 16)
                pool.wait_ge(skew_out, layer * 16 + 16)
                settle(pool)

            def attend(layer, s):
                it = layer * SEQS + s
                rows = s * SEQ
                n = 0
                for i in range(TILES + 2):
                    if i < TILES:
                        n += 1
                        powers(0, 1, n)
                    if i >= 2:
                        n += 1
                        powers(0, 6, n)
                pool.wait_ge(bias_in, it * 128 + 128)
                settle(pool)
                bias = bias_c[:, :, :, :].rearrange("p h m c -> p (h m) c")
                pool.tensor_tensor(bias, mask_c.unsqueeze(1).to_broadcast([P, 56, GRID]), bias, ALU.subtract)\
                    .then_inc(bias_ready, 1)
                for kind, i, k in schedule():
                    if kind == "slot" and KT <= k - SPLIT_FROM - 1 < 2 * KT:
                        split_out(pool, k - SPLIT_FROM - 1)
                    if kind == "heads_a":
                        n += 1
                        powers(0, 1, n)
                    if kind == "heads_b":
                        n += 1
                        powers(1, 2, n)
                    if kind == "norm":
                        n += 1
                        pool.wait_ge(x_new, i + 1)
                        pool.dma_start(x_d[bass.ds(rows + i * P, P), :], X[i][:, :]).then_inc(x_out, 16)
                        powers(3, 1, n)
                    if kind == "normed_0":
                        pool.wait_ge(xn_new, i + 1)
                        pool.dma_start(xn_d[bass.ds(rows + i * P, P), :], xn[:, :]).then_inc(xn_out, 16)
                        pool.wait_ge(x_out, it * 64 + (16 * i + 16))
                        settle(pool)
                pool.wait_ge(xn_out, it * 64 + 64)
                settle(pool)

            def gather(j):
                pool.indirect_dma_start(out=X[j][:, :], out_offset=None, in_=xn_d[:, :],
                                        in_offset=bass.IndirectOffsetOnAxis(ap=idx_in[j][:, 0:1], axis=0))\
                    .then_inc(gathered[j], 16)

            def experts(layer, g):
                for j in range(GROUP):
                    e = (g, j)
                    wait_e(pool, xe_turned, e, 2, 2)
                    wait_e(pool, idx_ready, e, 1, 1)
                    gather(j)
                    pool.wait_ge(scattered, (layer * GROUPS + g) * 64 + (16 * j + 16))
                    pool.sem_inc(added, 1)
                    wait_e(pool, y_scaled, e, 2, 2)
                    pool.indirect_dma_start(out=x_d[:, :],
                                            out_offset=bass.IndirectOffsetOnAxis(ap=idx_out[j][:, 0:1], axis=0),
                                            in_=xn[:, :] if j % 2 else nat[:, 0:D], in_offset=None,
                                            compute_op=ALU.add).then_inc(scattered, 16)

            with pool.Fori(0, LAYERS) as layer:
                prepare(layer)
                meet(layer * EPOCHS + 1)
                with pool.Fori(0, SEQS) as s:
                    attend(layer, s)
                    meet(layer * EPOCHS + s + 2)
                meet(layer * EPOCHS + 4)
                pool.sem_inc(added, AHEAD)
                pool.wait_ge(idx_first, 1)
                for j in range(GROUP):
                    gather(j)
                with pool.Fori(0, GROUPS) as g:
                    experts(layer, g)
                for j in range(GROUP):
                    pool.wait_ge(gathered[j], layer * 80 + 80)
                    settle(pool)
                meet(layer * EPOCHS + 5, quiet=True)
                pool.wait_ge(scattered, layer * 256 + 272)
                pool.sem_inc(x_there, 1)
            pool.dma_start(gate[:, :], g_final.rearrange("(a n) -> a n", a=1).to_broadcast([P, D])).then_inc(final_in, 16)
            for t in range(SEQS * TILES):
                powers(t, 1, t + 1)

        @block.scalar
        def _(act):
            act.wait_ge(started, 2)
            act.wait_ge(consts_in, 32)
            act.activation(nat[0:2, 0:D], nat[0:2, 0:D], ACT.Silu).then_inc(act_done, 1)
            act.wait_ge(c_turned, 1)
            act.activation(silu_c[:, :, :], bank[0][:, 0:KT * SEQS].rearrange("p (k s) -> p k s", s=SEQS),
                           ACT.Copy).then_inc(xn_ready, 1)
            act.wait_ge(slot_loaded[5], 16)
            for i in range(TILES):
                act.dma_start(X[i][:, :], x[i * P:(i + 1) * P, :]).then_inc(x_in[i], 16)

            def ada(layer):
                rows = hT[1][:, 0, :]
                for src, at, n in ((b_ada, R_BIAS, 48), (g_mix, R_GMIX, 8), (g_ffn, R_GFFN, 8), (g_grp, R_GGRP, 8)):
                    act.dma_start(rows[at:at + n, :], src[bass.ds(layer, 1), :].rearrange("o (k p) -> (o k) p", p=P))\
                        .then_inc(rows_in, 16)

            def spread_gate(dst, bank0):
                act.wait_ge(gate_turned, 1)
                act.activation(dst[:, 0:512], bank[bank0][:, :], ACT.Copy)
                act.activation(dst[:, 512:1024], bank[bank0 + 1][:, :], ACT.Copy).then_inc(gate_ready, 1)

            def attend(layer, s):
                it = layer * SEQS + s

                def normed(i):
                    act.wait_ge(vec_ready, 1)
                    if i >= 2:
                        act.wait_ge(proj_done, 4 * (i - 1))
                    for k in range(KT):
                        if k % 4 == 0:
                            act.wait_ge(h_turned, 2 * i + k // 4 + 1)
                        ins = act.activation(hT[i % 2][:, k, :], bank[k // 4][:, (k % 4) * P:(k % 4 + 1) * P],
                                             ACT.Identity, scale=vec[:, M_SC1 + k:M_SC1 + k + 1],
                                             bias=vec[:, M_SH1 + k:M_SH1 + k + 1])
                        if k % 4 == 3:
                            ins.then_inc(h_ready, 1)
                    for half in range(2):
                        act.wait_ge(h_ready, 2 * i + half + 1)
                        part_h = slice(4 * half, 4 * half + 4)
                        act.activation(h_hi[i % 2][:, part_h, :], hT[i % 2][:, part_h, :], ACT.Copy).then_inc(h_hi_ready, 1)

                def copies(i):
                    act.wait_ge(proj_done, projected(i, 2))
                    if i:
                        act.wait_ge(nat_ready, i)
                    act.activation(pbuf[:, 0, 256:384], bank[4][:, 0:128], ACT.Copy)
                    act.activation(V[:, i, 128:256], bank[4][:, 128:256], ACT.Copy)
                    if i:
                        act.wait_ge(qk_turned, 3 * i)
                    act.activation(nat[:, 768:1024], bank[4][:, 256:512], ACT.Copy).then_inc(proj_read_s, 1)
                    act.wait_ge(proj_done, projected(i, 3))
                    act.activation(nat[:, 1280:1536], bank[5][:, 0:256], ACT.Copy).then_inc(kc_ready, 1)
                    act.activation(V[:, i, 256:512], bank[5][:, 256:512], ACT.Copy).then_inc(proj_read_s, 1)

                def turned(i):
                    for n in range(3):
                        act.wait_ge(qk_turned, 3 * i + n + 1)
                        dst = qT[:, 4 * n:4 * n + 4, i * P:(i + 1) * P] if n < 2 else kT[:, :, i * P:(i + 1) * P]
                        act.activation(dst, bank[6 + n % 2][:, :].rearrange("p (a b) -> p a b", a=4), ACT.Copy,
                                       scale=-(HD ** -0.5) if n < 2 else 1.0).then_inc(qk_copied, 1)

                normed(0)
                for i in range(TILES):
                    if i + 1 < TILES:
                        normed(i + 1)
                    if i == 0:
                        for ch in (2, 3):
                            act.wait_ge(slot_loaded[ch], (layer * TURNS + s) * 16 + 48)
                            settle(act)
                            for kk in range(0, KT, 2):
                                act.activation(ring_r[2 + ch][:, kk:kk + 2, :], ring[ch][:, kk:kk + 2, :], ACT.Copy)\
                                    .then_inc(in_hi, 1)
                    if i:
                        turned(i - 1)
                    copies(i)
                turned(TILES - 1)

                side = 0
                for kind, i, k in schedule():
                    if kind == "slot":
                        if 0 <= k - SPLIT_FROM < 16:
                            half, kk = (k - SPLIT_FROM) // 8, (k - SPLIT_FROM) % 8
                            if kk == 0:
                                act.wait_ge(slot_loaded[4 + half], (layer * TURNS + s) * 16 + 48)
                                settle(act)
                            if k == SPLIT_FROM:
                                act.wait_ge(proj_done, 4 * TILES)
                            act.activation(ring_r[2 + half][:, kk, :], ring[4 + half][:, kk, :], ACT.Copy).then_inc(out_hi, 1)
                        if k < UNITS:
                            u = k % 16
                            grp, *_, st = unit(u)
                            n = keys(i, u)[1] * P
                            act.wait_ge(biased, k + 1)
                            src = bank[k % 3][:, 0:n] if grp == "B" else pbuf[:, k % 3, 0:n]
                            if k >= 3:
                                act.wait_ge(p_turned, k - 2)
                            act.activation(pbuf[:, k % 3, 0:n], src, ACT.Exp, scale=-1.0, bias=smin[:, i % 2, st:st + 1],
                                           accum_out=ssum[:, i % 2, st:st + 1]).then_inc(probs_ready, 1)
                        m = k - T_LAG
                        if 0 <= m < UNITS and m % 2 == 0:
                            n = keys(m // 16, m % 16)[1] * P
                            act.wait_ge(p_turned, m + 1)
                            if m >= 2:
                                act.wait_ge(pv_done, m - 1)
                            act.activation(pbuf[:, 3, 0:n], bank[3][:, 0:n], ACT.Copy).then_inc(pt_by_s, 1)
                    if kind == "sink":
                        act.wait_ge(sink_arg, i + 1)
                        act.activation(stat[:, 16:24], stat[:, 16:24], ACT.Exp).then_inc(sink_exp, 1)
                    if kind == "gate_copy":
                        spread_gate(gate, 6)
                    if kind in ("merged_0", "merged_1"):
                        half = int(kind[-1])
                        act.wait_ge(side_free, 7 * i + 1 + half)
                        if i:
                            act.wait_ge(side_full, 7 * (i - 1) + 4)
                        part_h = slice(4 * half, 4 * half + 4)
                        act.activation(merged_hi[:, part_h, :], hT[0][:, part_h, :], ACT.Copy).then_inc(merged_hi_ready, 1)
                    if kind in ("normed_0", "normed_1"):
                        half = int(kind[-1])
                        act.wait_ge(side_full, 7 * i + 5 + half)
                        for k4 in range(4):
                            kk = 4 * half + k4
                            ins = act.activation(hT[1][:, kk, :], bank[7][:, k4 * P:(k4 + 1) * P], ACT.Identity,
                                                 scale=vec[:, M_SC2 + kk:M_SC2 + kk + 1],
                                                 bias=vec[:, M_SH2 + kk:M_SH2 + kk + 1])
                        ins.then_inc(side_free, 1)
                    if kind == "router_1":
                        act.wait_ge(x_out, it * 64 + (16 * i + 16))
                        settle(act)
                        if i == 0:
                            act.wait_ge(scattered, layer * 256 + 16)
                            settle(act)
                        act.dma_start(X[i][:, :], x_d[bass.ds((s * -SEQ) + (SEQ + i * P), P), :]).then_inc(x_in[i], 16)

            def experts(layer, g):
                def hidden_copy(e, half):
                    wait_e(act, hid_turned, e, 2, half + 1)
                    if half == 0:
                        wait_e(act, y_done, e, 2, 0)
                    act.activation(hid_hi[:, 4 * half:4 * half + 4, :],
                                   bank[4 + half][:, :].rearrange("p (a b) -> p a b", a=4), ACT.Copy).then_inc(hid_copied, 1)

                for j in range(GROUP):
                    e = (g, j)
                    for half in range(2):
                        wait_e(act, gu_done, e, 4, 2 * half + 1)
                        act.sem_inc(slot_free[2 * half], 2)
                        wait_e(act, hid_ready, e, 2, half - 1)
                        act.activation(pbuf[:, half, :], bank[half][:, :], ACT.Silu).then_inc(silu_done, 1)
                        if half == 0:
                            for n in range(8):
                                if n % 4 == 0:
                                    act.wait_ge(slot_loaded[4 + n // 4], (layer * TURNS + g * GROUP) * 16 + (j + 3 + SEQS) * 16)
                                    settle(act)
                                kk = 2 * (n % 4)
                                act.activation(down_hi[n // 4][kk // 4][:, kk % 4:kk % 4 + 2, :], ring[4 + n // 4][:, kk:kk + 2, :],
                                               ACT.Copy).then_inc(down_hi_ready, 1)
                    hidden_copy(e, 0)
                    hidden_copy(e, 1)

            with act.Fori(0, LAYERS) as layer:
                ada(layer)
                barrier(act, layer * EPOCHS + 1)
                with act.Fori(0, SEQS) as s:
                    attend(layer, s)
                    barrier(act, layer * EPOCHS + s + 2)
                act.wait_ge(logit_max, 1)
                act.activation(probs_r, probs_r, ACT.Exp).then_inc(aff_exp, 1)
                spread_gate(gate, 2)
                for i in range(TILES):
                    act.wait_ge(x_in[i], layer * 48 + 48)
                    settle(act)
                barrier(act, layer * EPOCHS + 4)
                act.sem_inc(silu_done, AHEAD)
                act.sem_inc(hid_copied, AHEAD)
                act.sem_inc(down_hi_ready, AHEAD)
                with act.Fori(0, GROUPS) as g:
                    experts(layer, g)
                barrier(act, layer * EPOCHS + 5)
                act.wait_ge(x_there, layer + 1)
                settle(act)
                for i in range(TILES):
                    act.dma_start(X[i][:, :], x_d[i * P:(i + 1) * P, :]).then_inc(x_in[i], 16)
            for t in range(TILES, SEQS * TILES):
                act.dma_start(last[t], x_d[t * P:(t + 1) * P, :]).then_inc(last_in[t - TILES], 16)

        @block.vector
        def _(dve):
            for j in range(2, RING):
                dve.wait_ge(slot_loaded[j - 2], 16)
                dve.sem_inc(slot_free[j], 1)

            def ada(layer):
                chain = Chain(dve, dve_done)
                for n in range(12):
                    if n == 9:
                        dve.wait_ge(vec_turned, 1)
                        chain.add(dve.tensor_copy(rows_t[:, :], bank[0][:, 0:R_END]))
                    dve.wait_ge(ada_mm, n + 1)
                    if n >= 2:
                        dve.wait_ge(ada_turned, n - 1)
                    dve.tensor_copy(pbuf[0:2, n % 2, :], bank[2 + n % 2][0:2, :]).then_inc(ada_copied, 1)
                dve.wait_ge(layer_in, layer * 128 + 128)
                settle(dve)
                chain.add(dve.tensor_scalar(nsink[:, :], sinks[:, :], -1.0, None, ALU.mult))
                dve.wait_ge(ada_turned, 12)
                chain.add(dve.tensor_tensor(mods[:, :, :], bank[1][:, 0:M_END * SEQS].rearrange("p (m s) -> p m s", s=SEQS),
                                            bc(rows_t[:, R_BIAS:R_BIAS + M_END], SEQS), ALU.add))
                for sc, g in ((M_SC1, R_GMIX), (M_SC2, R_GFFN)):
                    dve.scalar_tensor_tensor(out=mods[:, sc:sc + 8, :], in0=mods[:, sc:sc + 8, :], scalar=1.0,
                                             in1=bc(rows_t[:, g:g + 8], SEQS), op0=ALU.add, op1=ALU.mult)

            def attend(layer, s):
                it = layer * SEQS + s
                chain = Chain(dve, dve_done)
                rn = [0]

                def rstd(count):
                    rn[0] += 1
                    dve.wait_ge(rstd_ready, rn[0])

                dve.tensor_copy(vec[:, :].unsqueeze(2), mods[:, :, bass.ds(s, 1)]).then_inc(vec_ready, 1)

                def norm(i):
                    dve.wait_ge(x_in[i], layer * 48 + s * 16 + 16)
                    if i:
                        dve.wait_ge(h_turned, 2 * i)
                    settle(dve)
                    dve.tensor_tensor_reduce(xn[:, :], X[i][:, :], X[i][:, :], 1.0 / D, EPS, ALU.mult, ALU.add,
                                             stat[:, 0:1]).then_inc(var_ready, 1)
                    rstd(1)
                    dve.tensor_scalar(xn[:, :], X[i][:, :], stat[:, 8:9], None, ALU.mult).then_inc(xn_ready, 1)

                def rotate(dst, src, cs, heads, half, t2):
                    a, b = src.shape[1], src.shape[2]
                    nb = HD // (2 * half)
                    cos = cs[:, 0:HD].unsqueeze(1).to_broadcast([P, b, HD])
                    for q in range(a):
                        chain.add(dve.tensor_tensor(dst[:, q], src[:, q], cos, ALU.mult))
                        for blk in range(nb):
                            o = blk * 2 * half
                            for lo, hi in ((o, o + half), (o + half, o)):
                                sin = cs[:, HD + lo:HD + lo + half].unsqueeze(1).to_broadcast([P, b, half])
                                ins = dve.tensor_tensor(t2[:, q, :, lo:lo + half], src[:, q, :, hi:hi + half], sin, ALU.mult)
                        chain.add(ins)
                        ins = dve.tensor_tensor(dst[:, q], dst[:, q], t2[:, q], ALU.add)
                    return ins

                def rope(i):
                    r0 = C_ROPE + 256 * i
                    ca, cb = con[:, r0:r0 + 128], con[:, r0 + 128:r0 + 256]
                    flat = pbuf[:, :, :].rearrange("p a b -> p (a b)")
                    t2 = flat[:, 512:1024].rearrange("p (a b d) -> p a b d", a=2, d=HD)
                    if i:
                        dve.wait_ge(qk_turned, 3 * i)
                    dve.wait_ge(proj_done, projected(i, 1))
                    chain.add(rotate(nat[:, 1024:1152].rearrange("p (a b d) -> p a b d", a=1, d=HD),
                                     bank[3][:, 0:128].rearrange("p (a b d) -> p a b d", a=1, d=HD), ca, 2, 32,
                                     flat[:, 512:640].rearrange("p (a b d) -> p a b d", a=1, d=HD)))
                    xb = flat[:, 0:384]
                    dve.tensor_copy(V[:, i, 0:128], bank[3][:, 128:256])
                    dve.tensor_copy(xb[:, 0:256], bank[3][:, 256:512]).then_inc(proj_read_v, 1)
                    dve.wait_ge(proj_read_v, 2 * i + 1)
                    dve.wait_ge(proj_read_s, 2 * i + 1)
                    sq = flat[:, 512:896]
                    xb3 = xb.rearrange("p (h d) -> p h d", d=HD)
                    chain.add(dve.tensor_tensor(sq, xb, xb, ALU.mult))
                    chain.add(dve.tensor_reduce(stat[:, 24:30], sq.rearrange("p (h d) -> p h d", d=HD), AX.X, ALU.add))
                    dve.tensor_scalar(stat[:, 0:6], stat[:, 24:30], 1.0 / HD, EPS, ALU.mult, ALU.add).then_inc(var_ready, 1)
                    rstd(6)
                    chain.add(dve.tensor_tensor(xb3, xb3, bc(stat[:, 8:14], HD), ALU.mult))
                    chain.add(dve.tensor_tensor(xb3, xb3, gain_b[:, :, :], ALU.mult))
                    chain.add(rotate(nat[:, 512:768].rearrange("p (j g d) -> p g j d", j=2, g=2),
                                     xb[:, 0:256].rearrange("p (g j d) -> p g j d", g=2, j=2), cb, 4, 16,
                                     flat[:, 512:768].rearrange("p (a b d) -> p a b d", a=2, d=HD)))
                    chain.add(rotate(nat[:, 1152:1280].rearrange("p (a b d) -> p a b d", a=1, d=HD),
                                     xb[:, 256:384].rearrange("p (a b d) -> p a b d", a=1, d=HD), cb, 2, 16,
                                     flat[:, 512:640].rearrange("p (a b d) -> p a b d", a=1, d=HD)))
                    dve.wait_ge(proj_done, projected(i, 0))
                    rotate(nat[:, 0:512].rearrange("p (j g d) -> p g j d", j=4, g=2),
                           bank[2][:, :].rearrange("p (g j d) -> p g j d", g=2, j=4), ca, 8, 32, t2).then_inc(nat_ready, 1)
                    dve.wait_ge(nat_ready, i + 1)
                    dve.sem_inc(proj_read_v, 1)

                def lower(i):
                    for half in range(2):
                        dve.wait_ge(h_hi_ready, 2 * i + half + 1)
                        part_h = slice(4 * half, 4 * half + 4)
                        dve.tensor_tensor(h_lo[i % 2][half][:, :, :], hT[i % 2][:, part_h, :],
                                          full(h_hi[i % 2][:, part_h, :]), ALU.subtract).then_inc(h_lo_ready, 1)

                norm(0)
                norm(1)
                lower(0)
                for i in range(TILES):
                    if i + 2 < TILES:
                        norm(i + 2)
                    if i + 1 < TILES:
                        lower(i + 1)
                    if i == 0:
                        for n in range(8):
                            dve.wait_ge(in_hi, n + 1)
                            ch, kk = 2 + n // 4, 2 * (n % 4)
                            dve.tensor_tensor(ring_r[ch][:, kk:kk + 2, :], ring[ch][:, kk:kk + 2, :],
                                              full(ring_r[2 + ch][:, kk:kk + 2, :]), ALU.subtract).then_inc(in_lo, 1)
                    rope(i)

                def ttr_min(out, in0, in1, first, acc):
                    return dve.tensor_tensor_reduce(out, in0, in1, 1.0, first, ALU.add, ALU.min, acc)

                for kind, i, k in schedule():
                    if kind == "slot":
                        if k < UNITS:
                            u = k % 16
                            grp, *_, st = unit(u)
                            lo, nb = keys(i, u)
                            dve.wait_ge(scored, k + 1)
                            if k >= 3:
                                dve.wait_ge(p_turned, k - 2)
                            src, dst, acc = bank[k % 3][:, 0:nb * P], pbuf[:, k % 3, 0:nb * P], smin[:, i % 2, st:st + 1]
                            if grp == "A":
                                off = (lo - (i - 1)) * P
                                ins = ttr_min(dst, src, mask_a[:, off:off + nb * P], nsink[:, st:st + 1], acc)
                            elif grp == "B":
                                ins = dve.tensor_reduce(acc, src, AX.X, ALU.min)
                            else:
                                if k == 12:
                                    dve.wait_ge(bias_ready, 1)
                                m = 7 - 2 * i - 1
                                ins = ttr_min(dst, src, bias_c[:, st - 12, m:m + NA_ROWS, :].rearrange("p m c -> p (m c)"),
                                              3e38, acc)
                            ins.then_inc(biased, 1)
                        m = k - T_LAG
                        if 0 <= m < UNITS and m % 2 == 1:
                            n = keys(m // 16, m % 16)[1] * P
                            dve.wait_ge(p_turned, m + 1)
                            if m >= 2:
                                dve.wait_ge(pv_done, m - 1)
                            dve.tensor_copy(pbuf[:, 4, 0:n], bank[4][:, 0:n]).then_inc(pt_by_v, 1)
                    if kind == "slot" and 0 <= k - SPLIT_FROM - 1 < KT:
                        split_out(dve, k - SPLIT_FROM - 1)
                    if kind in ("split_0", "split_1"):
                        half = int(kind[-1])
                        dve.wait_ge(merged_hi_ready, 2 * i + half + 1)
                        m = hT[0][:, 4 * half:4 * half + 4, :]
                        dve.tensor_tensor(merged_lo[:, 4 * half:4 * half + 4, :], m, full(merged_hi[:, 4 * half:4 * half + 4, :]),
                                          ALU.subtract)\
                            .then_inc(merged_lo_ready, 1)
                    if kind == "gate_columns":
                        dve.wait_ge(qk_turned, 3 * TILES)
                        dve.tensor_copy(nat[:, 0:D].rearrange("p (k m) -> p k m", m=P), bc(vec[:, M_GT1:M_GT1 + 8], P))\
                            .then_inc(gate_spread, 1)
                    if kind == "sink":
                        dve.wait_ge(biased, 16 * i + 8)
                        dve.tensor_tensor(stat[:, 16:24], smin[:, i % 2, 0:8], sinks[:, :], ALU.add).then_inc(sink_arg, 1)
                    if kind in ("heads_a", "heads_b"):
                        a = kind == "heads_a"
                        half = 0 if a else 1
                        dve.wait_ge(probs_ready, 16 * i + 8 * half + 8)
                        if a:
                            dve.wait_ge(sink_exp, i + 1)
                            chain.add(dve.tensor_tensor(ssum[:, i % 2, 0:8], ssum[:, i % 2, 0:8], stat[:, 16:24], ALU.add))
                        chain.add(dve.reciprocal(rinv[:, 8 * half:8 * half + 8], ssum[:, i % 2, 8 * half:8 * half + 8]))
                        dve.wait_ge(pv_done, 16 * i + 8 * half + 8)
                        if a and i == 0:
                            dve.wait_ge(gate_turned, 1)
                        if i and a:
                            dve.wait_ge(side_full, 7 * (i - 1) + 2)
                        cols = og[:, 512 * half:512 * half + 512]
                        dve.tensor_tensor(cols.rearrange("p (h d) -> p h d", d=HD),
                                          bank[5 + half][:, :].rearrange("p (h d) -> p h d", d=HD),
                                          bc(rinv[:, 8 * half:8 * half + 8], HD), ALU.mult).then_inc(heads_read, 1)
                        dve.wait_ge(heads_read, 2 * i + half + 1)
                        if i and a:
                            dve.wait_ge(side_full, 7 * (i - 1))
                        if i and not a:
                            dve.wait_ge(side_full, 7 * (i - 1) + 4)
                        junk = hT[1 if a else 0][:, :, :].rearrange("p a b -> p (a b)")
                        for n, (o, w) in enumerate(GROUP_COLS):
                            if (o < 512) == a:
                                ins = dve.tensor_tensor_reduce(junk[:, o:o + w], og[:, o:o + w], og[:, o:o + w], 1.0 / w, EPS,
                                                               ALU.mult, ALU.add, stat[:, n:n + 1])
                        ins.then_inc(var_ready, 1)
                        rn[0] += 1
                    if kind in ("scale_a", "scale_b"):
                        dve.wait_ge(rstd_ready, rn[0])
                        for n, (o, w) in enumerate(GROUP_COLS):
                            if (o < 512) == (kind == "scale_a"):
                                ins = dve.tensor_scalar(og[:, o:o + w], og[:, o:o + w], stat[:, 8 + n:9 + n], None, ALU.mult)
                        ins.then_inc(merged, 1)
                    if kind in ("merged_0", "merged_1"):
                        half = int(kind[-1])
                        dve.wait_ge(side_full, 7 * i + 1 + half)
                        dve.tensor_tensor(hT[0][:, 4 * half:4 * half + 4, :], bank[7][:, :].rearrange("p (a b) -> p a b", a=4),
                                          bc(rows_t[:, R_GGRP + 4 * half:R_GGRP + 4 * half + 4], P), ALU.mult)\
                            .then_inc(side_free, 1)
                    if kind in ("out_03", "out_13"):
                        half = int(kind[4])
                        cols = slice(512 * half, 512 * half + 512)
                        dve.wait_ge(side_full, 7 * i + 3 + half)
                        if i == 0:
                            dve.wait_ge(gate_ready, 1)
                        if i and not half:
                            dve.wait_ge(xn_out, it * 64 + 16 * i)
                            settle(dve)
                        dve.tensor_tensor(xn[:, cols], bank[7][:, :], gate[:, cols], ALU.mult).then_inc(side_free, 1)
                        dve.wait_ge(side_free, 7 * i + 3 + half)
                        chain.add(dve.tensor_tensor(X[i][:, cols], X[i][:, cols], xn[:, cols], ALU.add))
                        if half:
                            dve.sem_inc(x_new, 1)
                    if kind == "norm":
                        dve.tensor_tensor_reduce(xn[:, :], X[i][:, :], X[i][:, :], 1.0 / D, EPS, ALU.mult, ALU.add,
                                                 stat[:, 3:4]).then_inc(var_ready, 1)
                        rn[0] += 1
                    if kind == "normed":
                        dve.wait_ge(rstd_ready, rn[0])
                        dve.tensor_scalar(xn[:, :], X[i][:, :], stat[:, 11:12], None, ALU.mult).then_inc(xn_new, 1)
                    if kind == "router_1":
                        dve.wait_ge(side_full, 7 * i + 7)
                        dve.tensor_copy(aff[:, i, bass.ds(s, 1), 0:EXPERTS].rearrange("p o e -> p (o e)"),
                                        bank[7][:, 0:EXPERTS]).then_inc(side_free, 1)

            def route():
                chain = Chain(dve, dve_done)
                logits = aff[:, :, :, 0:EXPERTS].rearrange("p t s e -> p (t s) e")
                chain.add(dve.tensor_reduce(soft[:, 0, :], logits, AX.X, ALU.max))
                dve.tensor_tensor(probs_r, logits, bc(soft[:, 0, :], EXPERTS), ALU.subtract).then_inc(logit_max, 1)
                dve.wait_ge(aff_exp, 1)
                chain.add(dve.tensor_reduce(soft[:, 0, :], probs_r, AX.X, ALU.add))
                chain.add(dve.reciprocal(soft[:, 1, :], soft[:, 0, :]))
                dve.tensor_tensor(logits, probs_r, bc(soft[:, 1, :], EXPERTS), ALU.mult).then_inc(aff_ready, 1)
                dve.tensor_copy(nat[:, 0:D].rearrange("p (k m) -> p k m", m=64),
                                bc(mods[:, M_GT2:M_GT2 + 8, :].rearrange("p k s -> p (k s)"), 64)).then_inc(gate_spread, 1)
                dve.wait_ge(route_turned, 1)
                scores = hT[0][0:64, 0:4, :].rearrange("p a b -> p (a b)")
                sel = xn[0:64, 0:2 * CAP]
                found = pbuf[0:64, 0, 0:CAP].bitcast(u32)
                chain.add(dve.tensor_copy(scores, bank[0][0:64, :]))
                for r in range(CAP // 8):
                    top = sel[:, CAP + 8 * r:CAP + 8 * r + 8]
                    chain.add(dve.max(top, scores))
                    chain.add(dve.max_index(found[:, 8 * r:8 * r + 8], top, scores))
                    if r + 1 < CAP // 8:
                        chain.add(dve.match_replace(out=scores, in_to_replace=top, in_values=scores, imm_value=-1.0))
                dve.tensor_copy(sel[:, 0:CAP], found).then_inc(route_ready, 1)
                dve.wait_ge(route_turned, 2)
                b = bank[1]
                dve.tensor_copy(idx_f[0:64, :], b[0:64, 0:16])
                dve.tensor_scalar(idx_f[64:128, :], b[0:64, 32:48], float(SEQ), None, ALU.add)
                dve.tensor_copy(gate_t[0:64, :], b[64:128, 0:16])
                chain.add(dve.tensor_copy(gate_t[64:128, :], b[64:128, 32:48]))
                dve.memset(idx_t[:, EXPERTS:EXPERTS + GROUP], 0)
                chain.add(dve.tensor_copy(idx_t[:, 0:EXPERTS], idx_f[:, :]))

            def modulate(e, j):
                for half in range(2):
                    wait_e(dve, xe_turned, e, 2, half + 1)
                    if half == 0:
                        wait_e(dve, gu_done, e, 4, -4)
                    dst = hT[j % 2][:, 4 * half:4 * half + 4, :].rearrange("p k (s t) -> p (k s) t", s=SEQS)
                    a = mods[:, M_SC2 + 4 * half:M_SC2 + 4 * half + 4, :].rearrange("p k s -> p (k s)")
                    b = mods[:, M_SH2 + 4 * half:M_SH2 + 4 * half + 4, :].rearrange("p k s -> p (k s)")
                    dve.tensor_tensor(dst, bank[5 - half][:, :].rearrange("p (a b) -> p a b", a=8),
                                      bc(a, 64), ALU.mult).then_inc(xe_scaled, 1)
                    wait_e(dve, xe_scaled, e, 2, half + 1)
                    dve.tensor_tensor(dst, dst, bc(b, 64), ALU.add).then_inc(xe_ready, 1)

            def split_hidden(e, half):
                wait_e(dve, hid_copied, e, 2, half + 1)
                hi = hid_hi[:, 4 * half:4 * half + 4, :]
                dve.tensor_tensor(hid_lo[:, 4 * half:4 * half + 4, :], bank[4 + half][:, :].rearrange("p (a b) -> p a b", a=4),
                                  full(hi), ALU.subtract).then_inc(hid_split, 1)

            def experts(layer, g):
                for j in range(GROUP):
                    e = (g, j)
                    dve.wait_ge(gathered[j], (layer * (GROUPS + 1) + g) * 16 + 16)
                    settle(dve)
                    dve.tensor_copy(idx_in[j][:, 0:1], idx_t[:, bass.ds(g * GROUP + (j + GROUP), 1)])
                    dve.tensor_copy(idx_out[j][:, 0:1], idx_t[:, bass.ds(g * GROUP + j, 1)])
                    dve.tensor_copy(gate_now[:, j:j + 1], gate_t[:, bass.ds(g * GROUP + j, 1)]).then_inc(idx_ready, 1)
                    for half in range(2):
                        wait_e(dve, silu_done, e, 2, half + 1)
                        wait_e(dve, gu_done, e, 4, 2 * half + 2)
                        dve.sem_inc(slot_free[2 * half + 1], 2)
                        wait_e(dve, hid_turned, e, 2, half - 1)
                        dve.tensor_tensor(pbuf[:, 2 + half, :], pbuf[:, half, :], bank[2 + half][:, :], ALU.mult)\
                            .then_inc(hid_ready, 1)
                        if half == 0:
                            for n in range(8):
                                wait_e(dve, down_hi_ready, e, 8, n + 1)
                                kk = 2 * (n % 4)
                                dve.tensor_tensor(ring_r[4 + n // 4][:, kk:kk + 2, :], ring[4 + n // 4][:, kk:kk + 2, :],
                                                  full(down_hi[n // 4][kk // 4][:, kk % 4:kk % 4 + 2, :]), ALU.subtract)\
                                    .then_inc(down_lo_ready, 1)
                            split_hidden(e, 0)
                    modulate((g, j + 1), j + 1)
                    split_hidden(e, 1)
                    wait_e(dve, idx_ready, e, 1, 1)
                    wait_e(dve, added, e, 1, 0)
                    dst = xn if j % 2 else nat
                    for half in range(2):
                        wait_e(dve, y_done, e, 2, half + 1)
                        dve.sem_inc(slot_free[4 + half], 2)
                        dve.scalar_tensor_tensor(out=dst[:, 512 * half:512 * half + 512], in0=bank[6 + half][:, :],
                                                 scalar=gate_now[:, j:j + 1], in1=gate[:, 512 * half:512 * half + 512],
                                                 op0=ALU.mult, op1=ALU.mult).then_inc(y_scaled, 1)

            with dve.Fori(0, LAYERS) as layer:
                ada(layer)
                barrier(dve, layer * EPOCHS + 1)
                with dve.Fori(0, SEQS) as s:
                    attend(layer, s)
                    barrier(dve, layer * EPOCHS + s + 2)
                route()
                barrier(dve, layer * EPOCHS + 4)
                for j in range(GROUP):
                    ins = dve.tensor_copy(idx_in[j][:, 0:1], idx_t[:, j:j + 1])
                ins.then_inc(idx_first, 1)
                for done in (idx_ready, xe_scaled, xe_ready, hid_ready, y_scaled, down_lo_ready, hid_split):
                    dve.sem_inc(done, AHEAD)
                modulate((0, 0), 0)
                with dve.Fori(0, GROUPS) as g:
                    experts(layer, g)
                barrier(dve, layer * EPOCHS + 5)
            dve.wait_ge(final_in, 16)
            for t in range(SEQS * TILES + 1):
                if t < SEQS * TILES:
                    if t < TILES:
                        dve.wait_ge(x_in[t], 16 * (LAYERS * (SEQS + 1) + 1))
                    else:
                        dve.wait_ge(last_in[t - TILES], 16)
                    dve.tensor_tensor_reduce(xn[:, :] if t % 2 else nat[:, 0:D], last[t], last[t], 1.0 / D, EPS,
                                             ALU.mult, ALU.add, stat[:, t:t + 1]).then_inc(var_ready, 1)
                if t:
                    dve.wait_ge(rstd_ready, t)
                    dve.scalar_tensor_tensor(out=last[t - 1], in0=last[t - 1], scalar=stat[:, 7 + t:8 + t], in1=gate[:, :],
                                             op0=ALU.mult, op1=ALU.mult).then_inc(xn_new, 1)

        @block.tensor
        def _(pe):
            pe.wait_ge(consts_in, 32)
            for j in range(2):
                pe.sem_inc(slot_free[j], 1)
            pe.wait_ge(started, 2)
            pe.wait_ge(act_done, 1)
            for k in range(KT):
                ins = pe.transpose(bank[0][:, SEQS * k:SEQS * (k + 1)], nat[0:2, k * P:(k + 1) * P], ident[0:2, 0:2])
            ins.then_inc(c_turned, 1)
            pe.wait_ge(xn_ready, 1)

            def use(j, turn):
                pe.wait_ge(slot_loaded[j], turn * 16 + 16)
                settle(pe)

            def ada(layer):
                def turn_ada(n):
                    pe.wait_ge(ada_copied, n + 1)
                    for m in range(4):
                        o = SEQS * (4 * n + m)
                        ins = pe.transpose(bank[1][:, o:o + SEQS], pbuf[0:2, n % 2, m * P:(m + 1) * P], ident[0:2, 0:2])
                    ins.then_inc(ada_turned, 1)

                for n in range(12):
                    use(n % RING, layer * TURNS + n // RING)
                    if n >= 2:
                        pe.wait_ge(ada_copied, n - 1)
                    for k in range(KT):
                        ins = pe.matmul(bank[2 + n % 2][0:2, :], silu_c[:, k, :], ring[n % RING][:, k, :],
                                        start=(k == 0), stop=(k == KT - 1))
                    ins.then_inc(ada_mm, 1)
                    if n:
                        turn_ada(n - 1)
                        if n != 11:
                            pe.sem_inc(slot_free[(n - 1) % RING], 2)
                    if n == 8:
                        pe.wait_ge(rows_in, layer * 64 + 64)
                        settle(pe)
                        pe.transpose(bank[0][:, 0:R_END], hT[1][0:R_END, 0, :], ident[0:R_END, 0:R_END]).then_inc(vec_turned, 1)
                turn_ada(11)

            def spread_gate(bank0):
                pe.wait_ge(gate_spread, 1)
                for k in range(KT):
                    ins = pe.matmul(bank[bank0 + k // 4][:, (k % 4) * P:(k % 4 + 1) * P], nat[:, k * P:(k + 1) * P], ident,
                                    start=True, stop=True)
                ins.then_inc(gate_turned, 1)

            def attend(layer, s):
                it = layer * SEQS + s
                turn = layer * TURNS + s + 2

                def turn_h(i):
                    pe.wait_ge(xn_ready, i + 1)
                    for k in range(KT):
                        if k % 4 == 0 and i:
                            pe.wait_ge(h_ready, 2 * i - 1 + k // 4)
                        ins = pe.transpose(bank[k // 4][:, (k % 4) * P:(k % 4 + 1) * P], xn[:, k * P:(k + 1) * P], ident)
                        if k % 4 == 3:
                            ins.then_inc(h_turned, 1)

                def turn_qk(i):
                    pe.wait_ge(nat_ready, i + 1)
                    pe.wait_ge(kc_ready, i + 1)
                    for n in range(3):
                        if 3 * i + n >= 2:
                            pe.wait_ge(qk_copied, 3 * i + n - 1)
                        if n == 0 and i:
                            pe.wait_ge(qk_copied, 3 * i)
                        for a in range(4):
                            o = 512 * n + P * a
                            ins = pe.transpose(bank[6 + n % 2][:, a * P:(a + 1) * P], nat[:, o:o + P], ident)
                        ins.then_inc(qk_turned, 1)

                turn_h(0)
                for i in range(TILES):
                    if i + 1 < TILES:
                        turn_h(i + 1)
                    pe.wait_ge(h_ready, 2 * i + 2)
                    for ch in chunks(i):
                        split = ch >= 2
                        if split:
                            pe.wait_ge(in_lo, 4 * (ch - 1))
                            pe.wait_ge(h_lo_ready, 2 * i + 2)
                        elif i == 0:
                            use(ch, turn)
                        if i:
                            pe.wait_ge(proj_read_v if ch < 2 else proj_read_s, 2 * (i - 1) + (1, 0, 0, 1)[ch] + 1)
                        for k in range(KT):
                            out = bank[2 + ch][:, :]
                            if split:
                                hi, w_hi, w_lo = h_hi[i % 2][:, k, :], ring_r[2 + ch][:, k, :], ring_r[ch][:, k, :]
                                pe.matmul(out, hi, w_hi, start=(k == 0), stop=False)
                                pe.matmul(out, hi, w_lo, start=False, stop=False)
                                ins = pe.matmul(out, h_lo[i % 2][k // 4][:, k % 4, :], w_hi, start=False, stop=(k == KT - 1))
                            else:
                                ins = pe.matmul(out, hT[i % 2][:, k, :], ring[ch][:, k, :], start=(k == 0), stop=(k == KT - 1))
                        ins.then_inc(proj_done, 1)
                        if i and ch == chunks(i)[1]:
                            turn_qk(i - 1)
                pe.wait_ge(proj_done, 4 * TILES)
                for j in (0, 1, 4, 5):
                    pe.sem_inc(slot_free[j], 2)
                turn_qk(TILES - 1)
                pe.wait_ge(proj_read_v, 2 * TILES)
                pe.wait_ge(proj_read_s, 2 * TILES)
                pe.wait_ge(qk_copied, 3 * TILES)

                side = 0

                def side_turn(i):
                    if side:
                        pe.wait_ge(side_free, side)

                for kind, i, k in schedule():
                    if kind == "slot":
                        if k < UNITS:
                            grp, qp, g, kp, _, _, _ = unit(k % 16)
                            lo, nb = keys(i, k % 16)
                            if k >= 3:
                                pe.wait_ge(probs_ready, k - 2)
                            rows = slice(HD * g, HD * g + HD)
                            pe.matmul(bank[k % 3][:, 0:nb * P], qT[rows, qp, i * P:(i + 1) * P],
                                      kT[rows, kp, lo * P:(lo + nb) * P], start=True, stop=True).then_inc(scored, 1)
                        m = k - T_LAG
                        if 0 <= m < UNITS:
                            nb = keys(m // 16, m % 16)[1]
                            pe.wait_ge(probs_ready, m + 1)
                            if m >= 2:
                                pe.wait_ge(pt_by_v if m % 2 else pt_by_s, m // 2)
                            for b in range(nb):
                                ins = pe.transpose(bank[3 + m % 2][:, b * P:(b + 1) * P], pbuf[:, m % 3, b * P:(b + 1) * P], ident)
                            ins.then_inc(p_turned, 1)
                        m = k - V_LAG
                        if 0 <= m < UNITS:
                            _, _, _, _, vc, oc, _ = unit(m % 16)
                            lo, nb = keys(m // 16, m % 16)
                            pe.wait_ge(pt_by_v if m % 2 else pt_by_s, m // 2 + 1)
                            if m == 8:
                                pe.wait_ge(gate_ready, 1)
                            if m % 8 == 0 and m >= 16:
                                pe.wait_ge(heads_read, m // 8 - 1)
                            for b in range(nb):
                                ins = pe.matmul(bank[5 + oc // 512][:, oc % 512:oc % 512 + HD],
                                                pbuf[:, 3 + m % 2, b * P:(b + 1) * P], V[:, lo + b, vc:vc + HD],
                                                start=(b == 0), stop=(b == nb - 1))
                            ins.then_inc(pv_done, 1)
                    if kind == "gate_rows":
                        spread_gate(6)
                    if kind in ("merged_0", "merged_1"):
                        half = int(kind[-1])
                        side_turn(i)
                        pe.wait_ge(merged, 2 * i + 1 + half)
                        for a in range(4):
                            o = 512 * half + P * a
                            ins = pe.transpose(bank[7][:, a * P:(a + 1) * P], og[:, o:o + P], ident)
                        ins.then_inc(side_full, 1)
                        side += 1
                    if kind.startswith("out_"):
                        half, quarter = int(kind[4]), int(kind[5])
                        if quarter == 0:
                            side_turn(i)
                            if i == 0:
                                pe.wait_ge(out_lo[half], KT)
                        if quarter % 2 == 0:
                            pe.wait_ge(merged_lo_ready, 2 * i + 1 + quarter // 2)
                        for kk in range(2 * quarter, 2 * quarter + 2):
                            m_hi, m_lo = merged_hi[:, kk, :], merged_lo[:, kk, :]
                            w_hi, w_lo = ring_r[2 + half][:, kk, :], ring_r[4 + half][:, kk, :]
                            pe.matmul(bank[7][:, :], m_hi, w_hi, start=(kk == 0), stop=False)
                            pe.matmul(bank[7][:, :], m_hi, w_lo, start=False, stop=False)
                            ins = pe.matmul(bank[7][:, :], m_lo, w_hi, start=False, stop=(kk == KT - 1))
                        if quarter == 3:
                            ins.then_inc(side_full, 1)
                            side += 1
                    if kind in ("normed_0", "normed_1"):
                        half = int(kind[-1])
                        side_turn(i)
                        pe.wait_ge(xn_new, i + 1)
                        for a in range(4):
                            o = 512 * half + P * a
                            ins = pe.transpose(bank[7][:, a * P:(a + 1) * P], xn[:, o:o + P], ident)
                        ins.then_inc(side_full, 1)
                        side += 1
                    if kind in ("router_0", "router_1"):
                        half = int(kind[-1])
                        if not half:
                            side_turn(i)
                        for kk in range(4 * half, 4 * half + 4):
                            ins = pe.matmul(bank[7][:, 0:EXPERTS], hT[1][:, kk, :], router[:, kk, :],
                                            start=(kk == 0), stop=(kk == KT - 1))
                        if half:
                            ins.then_inc(side_full, 1)
                            side += 1
                pe.wait_ge(side_full, side)
                for j in range(2, 4):
                    pe.sem_inc(slot_free[j], 2)

            def route():
                pe.wait_ge(aff_ready, 1)
                for t in range(TILES):
                    ins = pe.transpose(bank[0][0:64, t * P:(t + 1) * P], aff[:, t, :, :].rearrange("p s e -> p (s e)"), ident)
                ins.then_inc(route_turned, 1)
                spread_gate(2)
                pe.wait_ge(route_ready, 1)
                pe.transpose(bank[1][:, 0:64], xn[0:64, 0:2 * CAP], ident[0:64, 0:64]).then_inc(route_turned, 1)

            def turn_xe(layer, e, j, half):
                if half == 0:
                    pe.wait_ge(gathered[j % GROUP], (layer * (GROUPS + 1) + e[0]) * 16 + (j // GROUP * 16 + 16))
                    settle(pe)
                wait_e(pe, hid_split, e, 2, -2 if half == 0 else -1)
                for a in range(4):
                    o = 512 * half + P * a
                    ins = pe.transpose(bank[5 - half][:, a * P:(a + 1) * P], X[j % GROUP][:, o:o + P], ident)
                ins.then_inc(xe_turned, 1)

            def experts(layer, g):
                def turn_hid(e, half):
                    wait_e(pe, hid_ready, e, 2, half + 1)
                    wait_e(pe, xe_ready, e, 2, 2 + half)
                    for a in range(4):
                        ins = pe.transpose(bank[4 + half][:, a * P:(a + 1) * P], pbuf[:, 2 + half, a * P:(a + 1) * P], ident)
                    ins.then_inc(hid_turned, 1)

                for j in range(GROUP):
                    e = (g, j)
                    turn = layer * TURNS + g * GROUP + (j + 2 + SEQS)
                    wait_e(pe, xe_ready, e, 2, 2)
                    for n in range(4):
                        half = n // 2
                        use(n, turn)
                        if n % 2 == 0:
                            wait_e(pe, hid_ready, e, 2, half - 1)
                        for k in range(KT):
                            ins = pe.matmul(bank[2 * (n % 2) + half][:, :], hT[j % 2][:, k, :], ring[n][:, k, :],
                                            start=(k == 0), stop=(k == KT - 1))
                        ins.then_inc(gu_done, 1)
                        if n == 2:
                            turn_hid(e, 0)
                            turn_xe(layer, (g, j + 1), j + 1, 0)
                    turn_xe(layer, (g, j + 1), j + 1, 1)
                    wait_e(pe, y_scaled, e, 2, 0)
                    wait_e(pe, hid_split, e, 2, 1)
                    for part_k in range(2):
                        if part_k:
                            wait_e(pe, hid_split, e, 2, 2)
                        for half in range(2):
                            if part_k == 0:
                                wait_e(pe, down_lo_ready, e, 8, 4 * half + 4)
                            for k in range(4 * part_k, 4 * part_k + 4):
                                w_hi, w_lo = down_hi[half][part_k][:, k % 4, :], ring_r[4 + half][:, k, :]
                                pe.matmul(bank[6 + half][:, :], hid_hi[:, k, :], w_hi, start=(k == 0), stop=False)
                                pe.matmul(bank[6 + half][:, :], hid_hi[:, k, :], w_lo, start=False, stop=False)
                                ins = pe.matmul(bank[6 + half][:, :], hid_lo[:, k, :], w_hi, start=False, stop=(k == KT - 1))
                            if part_k:
                                ins.then_inc(y_done, 1)
                            elif half == 0:
                                turn_hid(e, 1)

            with pe.Fori(0, LAYERS) as layer:
                ada(layer)
                barrier(pe, layer * EPOCHS + 1)
                with pe.Fori(0, SEQS) as s:
                    attend(layer, s)
                    barrier(pe, layer * EPOCHS + s + 2)
                pe.sem_inc(slot_free[4], 2)
                pe.sem_inc(slot_free[5], 2)
                route()
                barrier(pe, layer * EPOCHS + 4)
                for done in (xe_turned, gu_done, hid_turned, y_done):
                    pe.sem_inc(done, AHEAD)
                turn_xe(layer, (0, 0), 0, 0)
                turn_xe(layer, (0, 0), 0, 1)
                with pe.Fori(0, GROUPS) as g:
                    experts(layer, g)
                barrier(pe, layer * EPOCHS + 5)


def constants():
    import numpy as np
    f = np.float32
    out = np.zeros((P, C_END), f)
    out[:, C_ID:C_ID + P] = np.eye(P, dtype=f)
    q, k = np.arange(P)[:, None], np.arange(P)[None, :]
    out[:, C_MASKA:C_MASKA + P] = np.where(k >= q, 0, BIG)
    out[:, C_MASKA + 2 * P:C_MASKA + 3 * P] = np.where(k <= q, 0, BIG)
    col = np.arange(P)[:, None] % GRID
    start = np.clip(col - 8, 0, GRID - 16)
    kc = np.arange(GRID)[None, :]
    out[:, C_MASKC:C_MASKC + GRID] = np.where((kc >= start) & (kc < start + 16), 0, BIG)

    def table(pos, dim):
        inv = f(10000.0) ** (-np.arange(0, dim, 2, dtype=f) / f(dim))
        ang = pos.astype(f)[:, None] * inv[None, :].astype(f)
        return np.concatenate([np.cos(ang)] * 2, 1), np.concatenate([-np.sin(ang), np.sin(ang)], 1)

    t = np.arange(SEQ)
    ca, sa = table(t, HD)
    cr, sr = table(t // GRID, HD // 2)
    cc, sc = table(t % GRID, HD // 2)
    rope = np.concatenate([ca, sa, cr, cc, sr, sc], 1).astype(f)
    for i in range(TILES):
        out[:, C_ROPE + 256 * i:C_ROPE + 256 * (i + 1)] = rope[i * P:(i + 1) * P]
    return out


_NAMES = ["w_ada", "b_ada", "g_mix", "w_in", "sink", "q_gain", "k_gain", "rpb", "g_grp", "w_out", "g_ffn", "w_router",
          "w_gate", "w_up", "w_down", "g_final"]


def kernel(**inputs):
    import numpy as np
    import concourse.bacc as _bacc
    from concourse.bass_utils import run_bass_kernel_spmd as _run

    nc = _bacc.Bacc("TRN2", target_bir_lowering=False, num_devices=1)
    data = {
        "x": np.concatenate([np.asarray(inputs["x_prompt"]).reshape(SEQ, D), np.asarray(inputs["x_sample"]).reshape(SEQ, D)]),
        "c": np.concatenate([np.asarray(inputs["c_prompt"]), np.asarray(inputs["c_sample"])]),
    }
    for name in _NAMES:
        data[name] = np.ascontiguousarray(inputs[name])
    data["consts"] = constants()
    arrays, args = {}, []
    for name, a in data.items():
        arrays[f"in_{name}"] = a
        args.append(nc.dram_tensor(f"in_{name}", a.shape, mybir.dt.from_np(a.dtype), kind="ExternalInput").ap())
    args.append(nc.dram_tensor("out_y", (SEQS * SEQ, D), mybir.dt.float32, kind="ExternalOutput").ap())
    trunk(nc, *args)
    got = _run(nc, [arrays], core_ids=[0]).results[0]["out_y"]
    return got[0:SEQ].reshape(1, SEQ, D), got[SEQ:].reshape(1, SEQ, D)
```
